# Optimizing a Trainium2 kernel written in Bass

```python
import jax, jax.numpy as jnp
from jax import lax
import numpy as np

D_MODEL = 1024
BATCH = 1
SEQ = 256
DEPTH = 1
DEC_BATCH = 8
DEC_SEQ = 1
PAST_LEN = 2048
PAGE_SIZE = 128

N_META = 16
D_RNN = D_MODEL
N_GATE_BLOCKS = 16
GATE_BW = D_RNN // N_GATE_BLOCKS
CONV_W = 4
LRU_C = 8.0
N_HEADS = 16
HEAD_DIM = 64
N_KV = 2
GROUP = N_HEADS // N_KV
D_ATTN = N_HEADS * HEAD_DIM
D_KV = N_KV * HEAD_DIM
WINDOW = 128
BLOCK = 128
OFF_Q = D_RNN
OFF_K = OFF_Q + D_ATTN
OFF_V = OFF_K + D_KV
OFF_GR = OFF_V + D_KV
OFF_GA = OFF_GR + D_RNN
D_IN = OFF_GA + D_ATTN
D_MIX = D_RNN + D_ATTN
N_EXPERTS = 32
TOP_K = 4
D_FF = D_MODEL
SWIGLU_LIMIT = 7.0
SWIGLU_ALPHA = 1.702
MOE_BLOCK = 128
EPS = 1e-6

kernel_name = "hawk_swa_sink_moe_step"

def rmsnorm(x, g):
    xf = x.astype(jnp.float32)
    y = xf * lax.rsqrt(jnp.mean(xf * xf, axis=-1, keepdims=True) + EPS)
    return (y * g.astype(jnp.float32)).astype(x.dtype)

def alibi_slopes():
    return 2.0 ** (-8.0 * jnp.arange(1, N_HEADS + 1, dtype=jnp.float32) / N_HEADS)

def split_in(h, w_in):
    z = h @ w_in
    return (z[..., :OFF_Q], z[..., OFF_Q:OFF_K], z[..., OFF_K:OFF_V], z[..., OFF_V:OFF_GR], z[..., OFF_GR:OFF_GA], z[..., OFF_GA:D_IN])

def causal_conv(x_ext, w, b):
    T = x_ext.shape[1] - (CONV_W - 1)
    out = b
    for j in range(CONV_W):
        out = out + w[j] * x_ext[:, j:j + T]
    return out

def rg_lru(x, is_first, h0, w_rg, b_rg, w_ig, b_ig, lam):
    f32 = jnp.float32
    xf = x.astype(f32)
    xb = xf.reshape(xf.shape[:-1] + (N_GATE_BLOCKS, GATE_BW))
    r = jax.nn.sigmoid(jnp.einsum('btnc,ncd->btnd', xb, w_rg.astype(f32)).reshape(xf.shape) + b_rg.astype(f32))
    i = jax.nn.sigmoid(jnp.einsum('btnc,ncd->btnd', xb, w_ig.astype(f32)).reshape(xf.shape) + b_ig.astype(f32))
    log_a = -LRU_C * r * jax.nn.softplus(-lam.astype(f32))
    a = jnp.exp(log_a)
    mult = jnp.sqrt(-jnp.expm1(2.0 * log_a))
    mult = jnp.where(is_first[None, :, None], jnp.ones_like(mult), mult)
    b = mult * i * xf

    def step(h, inp):
        a_t, b_t = inp
        h_new = a_t * h + b_t
        return h_new, h_new

    h_last, hs = lax.scan(step, h0.astype(f32), (jnp.swapaxes(a, 0, 1), jnp.swapaxes(b, 0, 1)))
    return jnp.swapaxes(hs, 0, 1).astype(x.dtype), h_last

def window_attend(q, k, v, qpos, kpos, sinks):
    f32 = jnp.float32
    B, N, Q = q.shape[0], q.shape[1], q.shape[2]
    qg = q.reshape(B, N, Q, N_KV, GROUP, HEAD_DIM).astype(f32)
    s = jnp.einsum('bnqkgd,bnskd->bnkgqs', qg, k.astype(f32)) * (HEAD_DIM ** -0.5)
    dist = qpos[:, :, None] - kpos[:, None, :]
    mask = (kpos[:, None, :] >= 0) & (dist >= 0) & (dist < WINDOW)
    slopes = alibi_slopes().reshape(N_KV, GROUP)
    s = s - slopes[None, None, :, :, None, None] * dist.astype(f32)[None, :, None, None]
    s = jnp.where(mask[None, :, None, None], s, -jnp.inf)
    sink = jnp.broadcast_to(sinks.astype(f32).reshape(N_KV, GROUP)[None, None, :, :, None, None], s.shape[:-1] + (1,))
    p = jax.nn.softmax(jnp.concatenate([s, sink], axis=-1), axis=-1)[..., :-1]
    o = jnp.einsum('bnkgqs,bnskd->bnqkgd', p, v.astype(f32))
    return o.reshape(B, N, Q, D_ATTN).astype(q.dtype)

def to_blocks(t, pad_front, pad_end):
    tp = jnp.pad(t, ((0, 0), (pad_front, pad_end), (0, 0), (0, 0)))
    return tp.reshape((t.shape[0], -1, BLOCK) + tuple(t.shape[2:]))

def with_prev_block(tb):
    prev = jnp.concatenate([jnp.zeros_like(tb[:, :1]), tb[:, :-1]], axis=1)
    return jnp.concatenate([prev, tb], axis=2)

def merge_branches(y_rnn, y_attn, g_rnn, g_attn, w_out):
    m = jnp.concatenate([jax.nn.sigmoid(g_rnn) * y_rnn, jax.nn.sigmoid(g_attn) * y_attn], axis=-1)
    return m @ w_out

def moe(h, w_router, b_router, w_up, b_up, w_down, b_down):
    shp = h.shape
    t = h.reshape(-1, D_MODEL)
    T = t.shape[0]
    logits = (t @ w_router + b_router).astype(jnp.float32)
    top_v, top_i = lax.top_k(logits, TOP_K)
    wts = jax.nn.softmax(top_v, axis=-1)
    A = T * TOP_K
    flat_e = top_i.reshape(-1).astype(jnp.int32)
    flat_tok = jnp.arange(A, dtype=jnp.int32) // TOP_K
    flat_w = wts.reshape(-1)
    order = jnp.argsort(flat_e)
    e_sorted = flat_e[order]
    counts = jnp.zeros((N_EXPERTS,), jnp.int32).at[flat_e].add(1)
    padded = ((counts + (MOE_BLOCK - 1)) // MOE_BLOCK) * MOE_BLOCK
    ends = jnp.cumsum(padded).astype(jnp.int32)
    start_padded = ends - padded
    start_sorted = (jnp.cumsum(counts) - counts).astype(jnp.int32)
    rank = jnp.arange(A, dtype=jnp.int32) - start_sorted[e_sorted]
    dest = start_padded[e_sorted] + rank
    n_blk = -(-A // MOE_BLOCK) + N_EXPERTS
    n_rows = n_blk * MOE_BLOCK
    buf_tok = jnp.full((n_rows,), T, dtype=jnp.int32).at[dest].set(flat_tok[order])
    buf_w = jnp.zeros((n_rows,), jnp.float32).at[dest].set(flat_w[order])
    blk_start = jnp.arange(n_blk, dtype=jnp.int32) * MOE_BLOCK
    blk_expert = jnp.minimum(jnp.sum((ends[None, :] <= blk_start[:, None]).astype(jnp.int32), axis=1), N_EXPERTS - 1)
    t_pad = jnp.concatenate([t, jnp.zeros((1, D_MODEL), t.dtype)], axis=0)
    xin = t_pad[buf_tok].reshape(n_blk, MOE_BLOCK, D_MODEL)

    def run(args):
        xb, e = args
        z = xb @ w_up[e] + b_up[e]
        x_glu = jnp.minimum(z[:, ::2], SWIGLU_LIMIT)
        x_lin = jnp.clip(z[:, 1::2], -SWIGLU_LIMIT, SWIGLU_LIMIT)
        y = x_glu * jax.nn.sigmoid(SWIGLU_ALPHA * x_glu) * (x_lin + 1.0)
        return y @ w_down[e] + b_down[e]

    yb = lax.map(run, (xin, blk_expert)).reshape(n_rows, D_MODEL)
    out = jnp.zeros((T + 1, D_MODEL), jnp.float32).at[buf_tok].add(yb.astype(jnp.float32) * buf_w[:, None])[:T]
    return out.astype(h.dtype).reshape(shp)

def setup_inputs(seed: int = 0) -> dict:
    key = jax.random.key(seed)
    ks = jax.random.split(key, 28)
    f32 = jnp.float32

    def nrm(k, shape, scale):
        return jax.random.normal(k, shape, f32) * scale

    w_buf = min(WINDOW, PAST_LEN)
    a0 = jax.random.uniform(ks[15], (DEPTH, D_RNN), f32, 0.9, 0.999)
    return {
        "x_prompt": nrm(ks[0], (BATCH, SEQ, D_MODEL), 1.0),
        "x_sample": nrm(ks[1], (DEC_BATCH, DEC_SEQ, D_MODEL), 1.0),
        "cache_k": nrm(ks[2], (DEPTH, DEC_BATCH, w_buf, N_KV, HEAD_DIM), 1.0),
        "cache_v": nrm(ks[3], (DEPTH, DEC_BATCH, w_buf, N_KV, HEAD_DIM), 1.0),
        "state_conv": nrm(ks[4], (DEPTH, DEC_BATCH, CONV_W - 1, D_RNN), 1.0),
        "state_h": nrm(ks[5], (DEPTH, DEC_BATCH, D_RNN), 0.5),
        "meta_tokens": nrm(ks[6], (N_META, D_MODEL), 1.0),
        "norm_mix": 1.0 + nrm(ks[7], (DEPTH, D_MODEL), 0.02),
        "w_in": nrm(ks[8], (DEPTH, D_MODEL, D_IN), D_MODEL ** -0.5),
        "conv_w": nrm(ks[9], (DEPTH, CONV_W, D_RNN), CONV_W ** -0.5),
        "conv_b": nrm(ks[10], (DEPTH, D_RNN), 0.01),
        "w_rg": nrm(ks[11], (DEPTH, N_GATE_BLOCKS, GATE_BW, GATE_BW), GATE_BW ** -0.5),
        "b_rg": nrm(ks[12], (DEPTH, D_RNN), 0.01),
        "w_ig": nrm(ks[13], (DEPTH, N_GATE_BLOCKS, GATE_BW, GATE_BW), GATE_BW ** -0.5),
        "b_ig": nrm(ks[14], (DEPTH, D_RNN), 0.01),
        "lru_lambda": jnp.log(a0) - jnp.log1p(-a0),
        "attn_sinks": nrm(ks[16], (DEPTH, N_HEADS), 0.5),
        "w_out": nrm(ks[17], (DEPTH, D_MIX, D_MODEL), D_MIX ** -0.5),
        "norm_ffn": 1.0 + nrm(ks[18], (DEPTH, D_MODEL), 0.02),
        "w_router": nrm(ks[19], (DEPTH, D_MODEL, N_EXPERTS), D_MODEL ** -0.5),
        "b_router": nrm(ks[20], (DEPTH, N_EXPERTS), 0.01),
        "w_up": nrm(ks[21], (DEPTH, N_EXPERTS, D_MODEL, 2 * D_FF), D_MODEL ** -0.5),
        "b_up": nrm(ks[22], (DEPTH, N_EXPERTS, 2 * D_FF), 0.01),
        "w_down": nrm(ks[23], (DEPTH, N_EXPERTS, D_FF, D_MODEL), D_FF ** -0.5),
        "b_down": nrm(ks[24], (DEPTH, N_EXPERTS, D_MODEL), 0.01),
        "norm_final": 1.0 + nrm(ks[25], (D_MODEL,), 0.02),
    }

def reference(x_prompt, x_sample, cache_k, cache_v, state_conv, state_h, meta_tokens, norm_mix, w_in, conv_w, conv_b, w_rg, b_rg, w_ig, b_ig, lru_lambda, attn_sinks, w_out, norm_ffn, w_router, b_router, w_up, b_up, w_down, b_down, norm_final):
    B_p = x_prompt.shape[0]
    B_s, T_s = x_sample.shape[0], x_sample.shape[1]
    L = N_META + x_prompt.shape[1]
    xp = jnp.concatenate([jnp.broadcast_to(meta_tokens.astype(x_prompt.dtype)[None], (B_p, N_META, D_MODEL)), x_prompt], axis=1)
    xs = x_sample

    pad_front = (-N_META) % BLOCK
    pad_end = (-(pad_front + L)) % BLOCK
    Lp = pad_front + L + pad_end
    qpos_p = (jnp.arange(Lp, dtype=jnp.int32) - pad_front).reshape(Lp // BLOCK, BLOCK)
    kpos_p = jnp.concatenate([qpos_p - BLOCK, qpos_p], axis=1)
    first_p = jnp.arange(L, dtype=jnp.int32) == 0
    w_p = min(WINDOW, L)

    w_buf = cache_k.shape[2]
    qpos_s = (PAST_LEN + jnp.arange(T_s, dtype=jnp.int32))[None]
    kpos_s = jnp.concatenate([PAST_LEN - w_buf + jnp.arange(w_buf, dtype=jnp.int32), qpos_s[0]])[None]
    first_s = jnp.zeros((T_s,), dtype=bool)

    nk_p, nv_p, nc_p, nh_p = [], [], [], []
    nk_s, nv_s, nc_s, nh_s = [], [], [], []
    for l in range(DEPTH):
        h = rmsnorm(xp, norm_mix[l])
        xr, q, k, v, g_rnn, g_attn = split_in(h, w_in[l])
        conv_in = jnp.pad(xr, ((0, 0), (CONV_W - 1, 0), (0, 0)))
        y_rnn, h_last = rg_lru(causal_conv(conv_in, conv_w[l], conv_b[l]), first_p, jnp.zeros((B_p, D_RNN), jnp.float32), w_rg[l], b_rg[l], w_ig[l], b_ig[l], lru_lambda[l])
        k4 = k.reshape(B_p, L, N_KV, HEAD_DIM)
        v4 = v.reshape(B_p, L, N_KV, HEAD_DIM)
        qb = to_blocks(q.reshape(B_p, L, N_HEADS, HEAD_DIM), pad_front, pad_end)
        kw = with_prev_block(to_blocks(k4, pad_front, pad_end))
        vw = with_prev_block(to_blocks(v4, pad_front, pad_end))
        y_attn = window_attend(qb, kw, vw, qpos_p, kpos_p, attn_sinks[l]).reshape(B_p, Lp, D_ATTN)[:, pad_front:pad_front + L]
        xp = xp + merge_branches(y_rnn, y_attn, g_rnn, g_attn, w_out[l])
        xp = xp + moe(rmsnorm(xp, norm_ffn[l]), w_router[l], b_router[l], w_up[l], b_up[l], w_down[l], b_down[l])
        nk_p.append(k4[:, L - w_p:])
        nv_p.append(v4[:, L - w_p:])
        nc_p.append(conv_in[:, -(CONV_W - 1):])
        nh_p.append(h_last)

        h = rmsnorm(xs, norm_mix[l])
        xr, q, k, v, g_rnn, g_attn = split_in(h, w_in[l])
        conv_in = jnp.concatenate([state_conv[l].astype(xr.dtype), xr], axis=1)
        y_rnn, h_last = rg_lru(causal_conv(conv_in, conv_w[l], conv_b[l]), first_s, state_h[l], w_rg[l], b_rg[l], w_ig[l], b_ig[l], lru_lambda[l])
        k_all = jnp.concatenate([cache_k[l].astype(k.dtype), k.reshape(B_s, T_s, N_KV, HEAD_DIM)], axis=1)
        v_all = jnp.concatenate([cache_v[l].astype(v.dtype), v.reshape(B_s, T_s, N_KV, HEAD_DIM)], axis=1)
        y_attn = window_attend(q.reshape(B_s, 1, T_s, N_HEADS, HEAD_DIM), k_all[:, None], v_all[:, None], qpos_s, kpos_s, attn_sinks[l]).reshape(B_s, T_s, D_ATTN)
        xs = xs + merge_branches(y_rnn, y_attn, g_rnn, g_attn, w_out[l])
        xs = xs + moe(rmsnorm(xs, norm_ffn[l]), w_router[l], b_router[l], w_up[l], b_up[l], w_down[l], b_down[l])
        nk_s.append(k_all[:, -w_buf:])
        nv_s.append(v_all[:, -w_buf:])
        nc_s.append(conv_in[:, -(CONV_W - 1):])
        nh_s.append(h_last)

    y_prompt = rmsnorm(xp, norm_final)[:, N_META:]
    y_sample = rmsnorm(xs, norm_final)
    return (y_prompt, y_sample, jnp.stack(nk_p), jnp.stack(nv_p), jnp.stack(nc_p), jnp.stack(nh_p), jnp.stack(nk_s), jnp.stack(nv_s), jnp.stack(nc_s), jnp.stack(nh_s))


_drawn_inputs = setup_inputs


def setup_inputs(seed=0):
    import zlib

    import numpy as np

    out = dict(_drawn_inputs(seed))
    spreads = {}
    factors = {'b_rg': 25.01, 'b_ig': 12.166, 'b_up': 8.0, 'b_down': 8.0, 'norm_final': 7.877}
    for name, (base, spread) in spreads.items():
        noise = np.random.default_rng([zlib.crc32(name.encode()), seed]).standard_normal(out[name].shape)
        drawn = base * np.exp(spread * noise) if base else spread * noise
        out[name] = __import__('jax').numpy.asarray(drawn.astype(out[name].dtype))
    for name, factor in factors.items():
        out[name] = (out[name] * factor).astype(out[name].dtype)
    return out
```

```python
from collections import namedtuple
from contextlib import ExitStack

import numpy as np

import concourse.bass as bass
from concourse import mybir

F32 = mybir.dt.float32
BF16 = mybir.dt.bfloat16
I32 = mybir.dt.int32
U32 = mybir.dt.uint32
ALU = mybir.AluOpType
ACT = mybir.ActivationFunctionType
AX = mybir.AxisListType

P = 128
D = 1024
KB = D // P
SEQ, N_META, B_S = 256, 16, 8
L = SEQ + N_META
T = L + B_S
TAIL = T - 2 * P
TAIL_P = L - 2 * P
TILES = ((0, P), (P, P), (2 * P, TAIL))
CONV_W = 4
PAD = CONV_W - 1
N_HEADS, HEAD, N_KV = 16, 64, 2
GROUP = N_HEADS // N_KV
WINDOW = 128
OFF_Q, OFF_K = D, 2 * D
OFF_GR = OFF_K + 2 * N_KV * HEAD
OFF_GA = OFF_GR + D
E_N, TOP_K = 32, 4
LIMIT, ALPHA = 7.0, 1.702
EPS = 1e-6
LRU_C = 8.0
SLOPES = [2.0 ** (-8.0 * (h + 1) / N_HEADS) for h in range(N_HEADS)]

CAP = 64
PAIRS = E_N // 2
ROUNDS = -(-T // CAP)
NB = 512
RING = 16
SLOT = 2048
UP_SLOTS = 2 * KB
PAIR_SLOTS = UP_SLOTS + KB
HALF = RING // 2
COLS = 256
W_IN_ORDER = ([OFF_K] + [COLS * i for i in range(4)] + [OFF_GR + COLS * i for i in range(4)]
              + [OFF_Q + COLS * i for i in range(4)] + [OFF_GA + COLS * i for i in range(4)])
N_WIN, N_WOUT = len(W_IN_ORDER), D * 2 // P // 2
TRUNK = N_WIN + N_WOUT
BLK_XR, BLK_GR, BLK_Q, BLK_GA = 2, 2 + KB, 2 + 2 * KB, 2 + 3 * KB

C_ID, C_IOTA = 0, P
C_KEEP = P + CAP * ROUNDS
C_DQ = C_KEEP
C_D2 = C_DQ + 3 * P
KEYS2 = L - P
C_DD = C_D2 + KEYS2
C_TRI = C_DD + P
C_SEL = C_TRI + P
C_SL2 = C_SEL + E_N
C_SLD = C_SL2 + N_KV
C_OH2 = C_SLD + 1
C_OHD = C_OH2 + N_KV * N_HEADS
C_END = C_OHD + N_HEADS
MASKED = -1e30


def shape_constants():
    c = np.zeros((P, C_END), np.float32)
    row = np.arange(P)[:, None]
    c[:, C_ID:C_ID + P] = np.eye(P)
    c[:, C_IOTA:C_KEEP] = np.arange(CAP * ROUNDS)

    def distances(dist):
        return np.where((dist >= 0) & (dist < WINDOW), -dist, MASKED)

    c[:, C_DQ:C_DQ + P] = distances(row - np.arange(P))
    c[:, C_DQ + P:C_D2] = distances(P + row - np.arange(2 * P))
    c[:, C_D2:C_DD] = distances(P + row % TAIL_P - np.arange(KEYS2))
    c[:, C_DD:C_TRI] = -(WINDOW - 1 - np.arange(P))
    c[:, C_TRI:C_SEL] = row < np.arange(P)
    c[:, C_SEL:C_SL2] = row % E_N == np.arange(E_N)
    for kv in range(N_KV):
        head = GROUP * kv + 2 * (row[:, 0] % 64 // 16) + row[:, 0] // 64
        c[:, C_SL2 + kv] = np.array(SLOPES)[head]
        c[:, C_OH2 + N_HEADS * kv:C_OH2 + N_HEADS * (kv + 1)] = head[:, None] == np.arange(N_HEADS)
    head = row[:, 0] % N_HEADS
    c[:, C_SLD] = np.array(SLOPES)[head]
    c[:, C_OHD:C_END] = head[:, None] == np.arange(N_HEADS)
    return c


def expert_load(i):
    return (i % 2, i // 2) if i < UP_SLOTS else ((i - UP_SLOTS) % 2, (i - UP_SLOTS) // 2)


def ring_place(n):
    m = n + HALF
    slot = m % RING
    before = 0 if slot >= HALF else len(range(slot, TRUNK, HALF)) - 1
    return slot, m // RING, before


SEMS = """
x_loaded0 x_loaded1 x_loaded2 consts_loaded masks_loaded rows_loaded state_loaded sinks_loaded wgate_loaded
bias_loaded norm_loaded fnorm_loaded router_loaded cache_loaded newkv_loaded zeroed sums_zeroed squares mean_sq root
rstd_ready xhat_ready vec_tr vec_ready h_tr h_evac_a h_evac_v proj_done proj_evac xr_ready kv_tr kvtok_ready kd_tr
kd_ready state_tr state_ready conv_step conv_ready sp_in sp_exp sp_step gate_done gate_evac convout_tr convout_ready
kc_tr kc_ready decay_ready tanh_ready ix_ready var_ready mult_ready drive_ready rnn_gated bias_step score_done
biased rowmax negmax sink_exp exp_done denom rden p_scaled pt_done pt_evac_a pt_evac_v pv_done pv_evac qtok_tr
qtok_ready qd_tr qd_ready dsc_done dsc_ready dst_done q2_ready q2_done d_p_tr d_p_ready q2_p_tr q2_p_ready d_pv_done
d_pv_ready q2_pv_done q2_pv_ready sinkcol_step x_biased x_negmax x_sink_exp x_exp x_scaled ga_sig attn_gated
wout_used hout_tr hout_ready tail_moved x2_ready h2_ready h2_tr h2_evac logits_done negtop top_exp selb_ready
rank_done flag_ready cast_ready gather_oh weight_oh gather_done xt_ready up_done glu_ready lin_ready sig_ready
gated_ready y_ready ytr_done yt_ready gwt_tr gwt_ready down_done yd_ready combine_done added tail_copied tail_added
moe_done ring_used window_stored convout_stored hout_stored y_final stored router_step lru_step x_step
""".split()


def program(nc, c_in, x_prompt, x_sample, cache_k, cache_v, state_conv, state_h, meta_tokens, norm_mix, w_in, conv_w,
            conv_b, w_rg, b_rg, w_ig, b_ig, lru_lambda, attn_sinks, w_out, norm_ffn, w_router, b_router, w_up, b_up,
            w_down, b_down, norm_final,
            y_prompt, y_sample, new_k_p, new_v_p, new_conv_p, new_h_p, new_k_s, new_v_s, new_conv_s, new_h_s):
    ctx = ExitStack()
    with ctx:
        def sb(name, shape, dt=F32):
            return ctx.enter_context(nc.sbuf_tensor(name, shape, dt))

        s = namedtuple("Semaphores", SEMS)(*[ctx.enter_context(nc.semaphore(n)) for n in SEMS])
        ring_full = [ctx.enter_context(nc.semaphore(f"ring_full{i}")) for i in range(RING)]
        bank = [ctx.enter_context(nc.psum_tensor(f"bank{i}", [P, NB], F32)) for i in range(8)]

        ring = sb("ring", [P, RING, SLOT])
        x_tok = sb("x_tok", [P, 3, D])
        h_tok = sb("h_tok", [P, 3, D])
        keep = sb("keep", [P, C_KEEP])
        ident, iota = keep[:, C_ID:C_ID + P], keep[:, C_IOTA:C_KEEP]
        norm_b = sb("norm_b", [P, D])
        bias_parts = sb("bias_parts", [3 * E_N, 3 * D], BF16)
        pick = sb("pick", [3 * E_N, E_N, CAP], BF16)
        tri = sb("tri", [P, P], BF16)
        ones = sb("ones", [P, P], BF16)
        wr = sb("wr", [P, KB, E_N])
        br = sb("br", [P, E_N])
        vec = sb("vec", [P, 72])
        NRM, CW, CB, BR, BI, LAM = 0, 8, 40, 48, 56, 64
        decay = sb("decay", [P, 2 * KB])
        h0 = sb("h0", [P, KB, B_S])
        sinks = sb("sinks", [P, N_HEADS])
        stat = sb("stat", [P, 16])
        rank_m = sb("rank_m", [P, 3, E_N])
        wts = sb("wts", [P, 3, E_N])
        flag = sb("flag", [1, 1], I32)
        snk = sb("snk", [P, 4])

        area = sb("area", [P, (nc.sbuf_usable_end - nc.sbuf_base) // 4 // 8 * 8 - 8])
        used = [0]

        def at(base, shape, dt=F32, parts=P):
            size = int(np.prod(shape)) * (2 if dt == BF16 else 4) // 4
            v = area[0:parts, base:base + size]
            used[0] = max(used[0], base + size)
            if dt != F32:
                v = v.bitcast(dt)
            if len(shape) == 2:
                v = v.rearrange("p (a b) -> p a b", a=shape[0])
            elif len(shape) == 3:
                v = v.rearrange("p (a b c) -> p a b c", a=shape[0], b=shape[1])
            return v, base + size

        m_t, o = at(0, [2 * KB, T])
        kc, o = at(o, [B_S, P])
        vc, o = at(o, [B_S, P])
        kd, o = at(o, [N_KV, T])
        kt4, o = at(o, [3, 4 * HEAD])
        vt, o = at(o, [3, N_KV * HEAD])
        probs, o = at(o, [4, 3 * P])
        pt, o = at(o, [2, 3 * P])
        masks, o = at(o, [1, C_END - C_KEEP])
        q2z, o = at(o, [N_KV, P])
        qdz, o = at(o, [N_KV, GROUP * B_S])
        s_t, o = at(o, [1, P])
        p_d, o = at(o, [1, P])
        p_2, o = at(o, [N_KV, KEYS2])
        pt_d, o = at(o, [1, P])
        pt_2, o = at(o, [2 * N_KV, P])
        lru_tmp, o = at(o, [1, T])
        sm, o = at(o, [1, 64])
        masks, s_t, p_d, pt_d, lru_tmp, sm = (v[:, 0, :] for v in (masks, s_t, p_d, pt_d, lru_tmp, sm))
        st_in, o = at(0, [1, D])
        vec_in, o = at(o, [1, P])
        bias_in, o = at(o, [1, 3 * D])
        st_in, vec_in, bias_in = st_in[0:32, 0, :], vec_in[0:72, 0, :], bias_in[0:3 * E_N, 0, :]
        conv_out = probs[0:PAD + B_S, :, :].rearrange("p a b -> p (a b)")[:, 0:D]
        h2_t = m_t[:, 0:KB, :]
        o = 2 * KB * T
        lg, o = at(o, [3, E_N])
        top, o = at(o, [3, 8])
        topi, o = at(o, [3, 8], U32)
        topf, o = at(o, [3, TOP_K])
        ntop, o = at(o, [1, 4])
        tw, o = at(o, [3, TOP_K])
        tsum, o = at(o, [1, 4])
        eq, o = at(o, [3 * TOP_K, E_N])
        eqw, o = at(o, [3 * TOP_K, E_N])
        sel, o = at(o, [3, E_N])
        selb, o = at(o, [3, E_N], BF16)
        cnt, o = at(o, [1, 4])
        ntop, tsum = ntop[:, 0, :], tsum[:, 0, :]
        o = 2 * KB * T + 2048
        g_oh, o = at(o, [3, P])
        gw0, o = at(o, [3, P])
        gw1, o = at(o, [3, P])
        xe, o = at(o, [KB, P])
        gw_t, o = at(o, [1, T])
        glu, o = at(o, [2, COLS])
        lin, o = at(o, [2, COLS])
        sig, o = at(o, [2, COLS])
        o = 0
        y_e, o = at(o, [1, D])
        y_t, o = at(o, [KB, P])
        yd, o = at(o, [1, D])
        y_e, yd, gw_t = y_e[:, 0, :], yd[:, 0, :], gw_t[:, 0, :]
        tail_sb, o = at(o, [1, NB])
        tail_sb = tail_sb[:, 0, :]
        gw = (gw0, gw1)

        upper = ring[:, HALF:RING, :].rearrange("p a b -> p (a b)")
        o = 0

        def up(n, words=T):
            nonlocal o
            v = upper[:, o:o + n * words].rearrange("p (a b) -> p a b", a=n)
            o += n * words
            return v

        xr = up(KB, PAD + T)
        q_t = upper[:, 0:KB * T].rearrange("p (a b) -> p a b", a=KB)
        sdec = up(KB, PAD * B_S)
        g_r, g_a, xc, a_t, b_t, h_t = (up(KB) for _ in range(6))
        kv_t = g_a[:, 0:2, :]
        tanh_t = g_a
        wblk = h_tok[:, 0:2, :].rearrange("p a (j c) -> p a j c", j=KB)
        kc_t = h_tok[:, 2, :].rearrange("p (b c) -> p b c", b=B_S)
        q_tok = h_tok[0:B_S, 0, :].rearrange("p (g k d) -> p g k d", g=GROUP, k=N_KV)
        h_out = h_tok[0:1 + B_S, 1, :]

        win_v = w_in[0].rearrange("(k p) c -> p k c", p=P)
        wout_v = w_out[0].rearrange("(g j p) c -> g p j c", p=P, j=2)
        wup_v = w_up[0].rearrange("e (k p) c -> e k p c", p=P)
        wdn_v = w_down[0].rearrange("e (g j p) c -> e g p j c", p=P, j=2)

        def rows(t):
            return TILES[t][1]

        def msk(lo, n):
            return masks[:, lo - C_KEEP:lo - C_KEEP + n]

        def h2_bank(t, half):
            return bank[((5, 6), (0, 1), (7, 4))[t][half]][:, 0:4 * rows(t)]

        lg_bank = (bank[2], bank[5], bank[6])

        block = ctx.enter_context(nc.Block())

        @block.sync
        def _(eng):
            eng.dma_start(x_tok[0:N_META, 0, :], meta_tokens).then_inc(s.x_loaded0, 16)
            eng.dma_start(x_tok[N_META:P, 0, :], x_prompt[0, 0:P - N_META, :]).then_inc(s.x_loaded0, 16)
            eng.dma_start(x_tok[:, 1, :], x_prompt[0, P - N_META:2 * P - N_META, :]).then_inc(s.x_loaded1, 16)
            eng.dma_start(x_tok[0:TAIL_P, 2, :], x_prompt[0, 2 * P - N_META:SEQ, :]).then_inc(s.x_loaded2, 16)
            eng.dma_start(x_tok[TAIL_P:TAIL, 2, :], x_sample.rearrange("b o d -> (b o) d")).then_inc(s.x_loaded2, 16)
            for n in range(TRUNK):
                if n >= HALF:
                    eng.wait_ge(s.proj_done, 2 * (n - HALF) + 2)
                if n < N_WIN:
                    dst = ring[:, n % HALF, :].rearrange("p (k c) -> p k c", k=KB)
                    src = win_v[:, :, W_IN_ORDER[n]:W_IN_ORDER[n] + COLS]
                else:
                    dst = ring[:, n % HALF, :].rearrange("p (j c) -> p j c", j=2)
                    src = wout_v[n - N_WIN]
                eng.dma_start(dst, src).then_inc(ring_full[n % HALF], 16)
                if n == 10:
                    eng.wait_ge(s.kvtok_ready, 6)
                    for cache, tok, new in ((kc, kt4, new_k_p), (vc, vt, new_v_p)):
                        w = tok.rearrange("p t (k r) -> p t k r", k=N_KV)
                        first = L - WINDOW - P
                        out = new[0, 0]
                        for kv in range(N_KV):
                            eng.dma_start(out[0:P - first, kv, :], w[first:P, 1, kv, 0:HEAD]).then_inc(s.stored, 16)
                            eng.dma_start(out[P - first:WINDOW, kv, :], w[0:TAIL_P, 2, kv, 0:HEAD]).then_inc(s.stored, 16)
                            eng.dma_start(cache[WINDOW - 1:WINDOW, :, HEAD * kv:HEAD * (kv + 1)],
                                          w[TAIL_P:TAIL, 2, kv, 0:HEAD]).then_inc(s.newkv_loaded, 16)

            def expert_dma(expert, i, slot):
                part = expert_load(i)[1]
                if i < UP_SLOTS:
                    eng.dma_start(ring[:, slot, :], wup_v[expert, part]).then_inc(ring_full[slot], 16)
                else:
                    eng.dma_start(ring[:, slot, :].rearrange("p (j c) -> p j c", j=2),
                                  wdn_v[expert, part]).then_inc(ring_full[slot], 16)

            eng.wait_ge(s.attn_gated, KB)
            eng.wait_ge(s.rnn_gated, 1)
            eng.wait_ge(s.hout_tr, 2)
            for n in range(2 * PAIR_SLOTS):
                slot, turn, _ = ring_place(n)
                if HALF <= n < RING:
                    last = [m for m in range(TRUNK) if m % HALF == slot][-1]
                    eng.wait_ge(s.wout_used, last - N_WIN + 1)
                elif n >= RING:
                    eng.wait_ge(s.ring_used, n - RING + 1)
                expert_dma(2 * (n // PAIR_SLOTS) + expert_load(n % PAIR_SLOTS)[0], n % PAIR_SLOTS, slot)
                if n == RING:
                    eng.dma_start(norm_b[:, :], norm_final.rearrange("(o d) -> o d", o=1).to_broadcast([P, D]))\
                       .then_inc(s.fnorm_loaded, 16)
            with eng.Fori(1, PAIRS // 2) as it:
                for n in range(2 * PAIR_SLOTS):
                    slot = ring_place(n)[0]
                    eng.wait_ge(s.ring_used, 2 * PAIR_SLOTS * it + (n - RING + 1))
                    expert_dma(4 * it + 2 * (n // PAIR_SLOTS) + expert_load(n % PAIR_SLOTS)[0], n % PAIR_SLOTS, slot)

            eng.wait_ge(s.flag_ready, 1)
            more = eng.value_load(flag[0:1, 0:1], min_val=0, max_val=1)
            with eng.If(more > 0):
                with eng.Fori(1, ROUNDS) as rnd:
                    with eng.Fori(0, PAIRS // 2) as it:
                        for n in range(2 * PAIR_SLOTS):
                            slot = ring_place(n)[0]
                            eng.wait_ge(s.ring_used, PAIR_SLOTS * PAIRS * rnd + 2 * PAIR_SLOTS * it + (n - RING + 1))
                            expert_dma(4 * it + 2 * (n // PAIR_SLOTS) + expert_load(n % PAIR_SLOTS)[0],
                                       n % PAIR_SLOTS, slot)
            for t in range(3):
                eng.wait_ge(s.y_final, t + 1)
                if t == 0:
                    eng.dma_start(y_prompt[0, 0:P - N_META, :], h_tok[N_META:P, 0, :]).then_inc(s.stored, 16)
                elif t == 1:
                    eng.dma_start(y_prompt[0, P - N_META:2 * P - N_META, :], h_tok[:, 1, :]).then_inc(s.stored, 16)
                else:
                    eng.dma_start(y_prompt[0, 2 * P - N_META:SEQ, :], h_tok[0:TAIL_P, 2, :]).then_inc(s.stored, 16)
                    eng.dma_start(y_sample.rearrange("b o d -> (b o) d"), h_tok[TAIL_P:TAIL, 2, :]).then_inc(s.stored, 16)
            eng.wait_ge(s.stored, 16 * (8 + 1 + 4))
            eng.wait_ge(s.window_stored, 32)
            eng.wait_ge(s.convout_stored, 32)
            eng.wait_ge(s.hout_stored, 32)

        @block.gpsimd
        def _(eng):
            eng.memset(ones[:, :], 1.0).then_inc(s.zeroed, 1)
            eng.memset(xr[:, :, 0:PAD], 0.0).then_inc(s.zeroed, 1)
            eng.memset(q2z[:, :, :], 0.0).then_inc(s.zeroed, 1)
            eng.memset(qdz[:, :, :], 0.0).then_inc(s.zeroed, 1)
            eng.wait_ge(s.h_tr, KB)
            eng.memset(h_tok[:, 0:2, :], 0.0).then_inc(s.zeroed, 1)
            eng.wait_ge(s.bias_loaded, 16 * 6)
            n = 0
            for part in range(3):
                r = slice(E_N * part, E_N * (part + 1))
                for step in range(part + 1):
                    if n:
                        eng.wait_ge(s.bias_step, n)
                    eng.tensor_copy(bias_parts[r, :], bias_in[r, :]).then_inc(s.bias_step, 1)
                    n += 1
                    if step < part:
                        eng.wait_ge(s.bias_step, n)
                        eng.tensor_tensor(bias_in[r, :], bias_in[r, :], bias_parts[r, :], ALU.subtract)\
                           .then_inc(s.bias_step, 1)
                        n += 1
            eng.wait_ge(s.bias_step, 9)
            for j in range(KB):
                eng.wait_ge(s.gate_evac, 2 * j + 2)
                eng.wait_ge(s.ix_ready, j)
                eng.tensor_tensor(b_t[:, j, :], b_t[:, j, :], xc[:, j, :], ALU.mult).then_inc(s.ix_ready, 1)
            eng.wait_ge(s.ix_ready, KB)
            for j in range(KB):
                for p in range(2):
                    buf = probs[:, 2 * (j % 2) + p, :]
                    rd = sm[:, 16 * (j % 2) + 8 * p + 6:16 * (j % 2) + 8 * p + 8]
                    eng.wait_ge(s.rden, 2 * j + p + 1)
                    eng.wait_ge(s.p_scaled, 4 * j + 2 * p)
                    eng.tensor_scalar(buf[:, 0:P], buf[:, 0:P], rd[:, 0:1], None, ALU.mult).then_inc(s.p_scaled, 1)
                    eng.wait_ge(s.p_scaled, 4 * j + 2 * p + 1)
                    eng.tensor_scalar(buf[:, P:3 * P], buf[:, P:3 * P], rd[:, 1:2], None, ALU.mult)\
                       .then_inc(s.p_scaled, 1)

        @block.scalar
        def _(eng):
            act = eng.activation
            eng.dma_start(keep[:, :], c_in[:, 0:C_KEEP]).then_inc(s.consts_loaded, 16)
            for i, (v, n) in enumerate(((norm_mix, 1), (conv_w, 4), (conv_b, 1), (b_rg, 1), (b_ig, 1), (lru_lambda, 1))):
                first = (0, 8, 40, 48, 56, 64)[i]
                flat = v.rearrange("o (j c) -> (o j) c", c=P) if n == 1 else v.rearrange("o w (j c) -> (o w j) c", c=P)
                eng.dma_start(vec_in[first:first + KB * n, :], flat).then_inc(s.rows_loaded, 16)
            eng.wait_ge(s.sums_zeroed, 1)
            for t in range(3):
                eng.wait_ge((s.x_loaded0, s.x_loaded1, s.x_loaded2)[t], 32 if t != 1 else 16)
                act(h_tok[0:rows(t), t, :], x_tok[0:rows(t), t, :], ACT.Square, accum_out=stat[0:rows(t), t:t + 1])\
                    .then_inc(s.squares, 1)
            eng.wait_ge(s.mean_sq, 1)
            act(stat[:, 6:9], stat[:, 3:6], ACT.Sqrt).then_inc(s.root, 1)
            eng.dma_start(masks[:, :], c_in[:, C_KEEP:C_END]).then_inc(s.masks_loaded, 16)
            eng.dma_start(st_in[0:PAD * B_S, :], state_conv.rearrange("o b r d -> (o b r) d")).then_inc(s.state_loaded, 16)
            eng.dma_start(st_in[PAD * B_S:32, :], state_h[0]).then_inc(s.state_loaded, 16)
            for part in range(3):
                eng.dma_start(bias_in[E_N * part:E_N * (part + 1), 0:2 * D], b_up[0]).then_inc(s.bias_loaded, 16)
                eng.dma_start(bias_in[E_N * part:E_N * (part + 1), 2 * D:], b_down[0]).then_inc(s.bias_loaded, 16)
            for cache, src in ((kc, cache_k), (vc, cache_v)):
                eng.dma_start(cache[0:WINDOW - 1, :, :], src[0, :, 1:WINDOW].rearrange("b r k d -> r b (k d)"))\
                   .then_inc(s.cache_loaded, 16)
            eng.dma_start(sinks[:, :], attn_sinks.to_broadcast([P, N_HEADS])).then_inc(s.sinks_loaded, 16)
            eng.dma_start(norm_b[:, :], norm_ffn.to_broadcast([P, D])).then_inc(s.norm_loaded, 16)
            eng.dma_start(wr[:, :, :], w_router[0].rearrange("(k p) e -> p k e", p=P)).then_inc(s.router_loaded, 16)
            eng.dma_start(br[:, :], b_router.to_broadcast([P, E_N])).then_inc(s.router_loaded, 16)
            eng.wait_ge(s.vec_ready, 1)
            for j in range(0, KB, 2):
                eng.wait_ge(s.h_tr, j + 1)
                act(h_t[:, j, :], bank[j][:, 0:T], ACT.Copy, scale=vec[:, NRM + j:NRM + j + 1]).then_inc(s.h_evac_a, 1)
            eng.wait_ge(s.sp_in, 1)
            act(sm[:, 8:16], sm[:, 0:8], ACT.Exp).then_inc(s.sp_exp, 1)
            eng.wait_ge(s.zeroed, 5)
            for g, w in ((0, w_rg), (1, w_ig)):
                for half in range(2):
                    eng.dma_start(wblk[64 * half:64 * half + 64, g, :, 64 * half:64 * half + 64],
                                  w[0].rearrange("(j h) c d -> h c j d", h=2)[half]).then_inc(s.wgate_loaded, 16)

            def evac(n, dst, **kw):
                eng.wait_ge(s.proj_done, n + 1)
                return act(dst, bank[n % 2][:, 0:T], kw.pop("func", ACT.Copy), **kw)

            evac(0, kv_t[:, 0, :]).then_inc(s.proj_evac, 1)
            evac(1, kv_t[:, 1, :]).then_inc(s.proj_evac, 1)
            eng.wait_ge(s.zeroed, 2)
            for j in range(KB):
                evac(BLK_XR + j, xr[:, j, PAD:PAD + T]).then_inc(s.xr_ready, 1)
                act(xc[:, j, :], bank[j % 2][:, 0:T], ACT.Identity, bias=vec[:, CB + j:CB + j + 1],
                    scale=vec[:, CW + 8 * PAD + j:CW + 8 * PAD + j + 1]).then_inc(s.proj_evac, 1)
                if j == 2:
                    for kv in range(N_KV):
                        eng.wait_ge(s.kd_tr, kv + 1)
                        act(kd[:, kv, :], bank[6 + kv][:, 0:T], ACT.Copy).then_inc(s.kd_ready, 1)
            for j in range(KB):
                evac(BLK_GR + j, g_r[:, j, :], func=ACT.Sigmoid).then_inc(s.proj_evac, 1)
                for g, (dst, b) in enumerate(((a_t, BR), (b_t, BI))):
                    eng.wait_ge(s.gate_done, 2 * j + g + 1)
                    act(dst[:, j, :], bank[4 + g][:, 0:T], ACT.Sigmoid, bias=vec[:, b + j:b + j + 1])\
                        .then_inc(s.gate_evac, 1)
                if j == 5 or j == 6:
                    half = j - 5
                    eng.wait_ge(s.kc_tr, half + 1)
                    act(kc_t[:, 4 * half:4 * half + 4, :].rearrange("p b c -> p (b c)"), bank[6 + half][:, :], ACT.Copy)\
                        .then_inc(s.kc_ready, 1)
            eng.wait_ge(s.convout_ready, 2)
            eng.dma_start(new_conv_p[0, 0], conv_out[0:PAD, :]).then_inc(s.convout_stored, 16)
            eng.dma_start(new_conv_s[0, :, PAD - 1, :], conv_out[PAD:PAD + B_S, :]).then_inc(s.convout_stored, 16)
            eng.dma_start(new_conv_s[0, :, 0:PAD - 1, :], state_conv[0, :, 1:PAD, :]).then_inc(s.stored, 16)
            eng.wait_ge(s.cache_loaded, 32)
            eng.wait_ge(s.newkv_loaded, 64)
            for cache, new in ((kc, new_k_s), (vc, new_v_s)):
                eng.dma_start(new[0].rearrange("b r k d -> r b (k d)"), cache[:, :, :]).then_inc(s.window_stored, 16)
            eng.wait_ge(s.gate_evac, 2 * KB)

            def attention_exp(j):
                for p in range(2):
                    col = 16 * (j % 2) + 8 * p
                    h = 2 * j + p
                    eng.wait_ge(s.negmax, h + 1)
                    act(sm[:, col + 4:col + 6], sm[:, col + 2:col + 4], ACT.Exp, bias=sinks[:, h:h + 1])\
                        .then_inc(s.sink_exp, 1)
                    buf = probs[:, 2 * (j % 2) + p, :]
                    for i, (lo, hi) in enumerate(((0, P), (P, 3 * P))):
                        act(buf[:, lo:hi], buf[:, lo:hi], ACT.Exp, bias=sm[:, col + 2 + i:col + 3 + i],
                            accum_out=sm[:, col + i:col + i + 1]).then_inc(s.exp_done, 1)

            def extra_exp(n, buf, width):
                col = 32 + 6 * n
                eng.wait_ge(s.x_negmax, n + 1)
                act(sm[:, col + 2:col + 3], sm[:, col + 1:col + 2], ACT.Exp, bias=snk[:, n:n + 1])\
                    .then_inc(s.x_sink_exp, 1)
                act(buf[:, 0:width], buf[:, 0:width], ACT.Exp, bias=sm[:, col + 1:col + 2],
                    accum_out=sm[:, col:col + 1]).then_inc(s.x_exp, 1)

            for st in range(2 * KB):
                j = st % KB
                if st < 2:
                    for i in range(4 * st, 4 * st + 4):
                        act(tanh_t[:, i, :], a_t[:, i, :], ACT.Tanh, scale=decay[:, i:i + 1]).then_inc(s.tanh_ready, 1)
                        eng.wait_ge(s.tanh_ready, i + 1)
                        act(a_t[:, i, :], a_t[:, i, :], ACT.Exp, scale=decay[:, KB + i:KB + i + 1]).then_inc(s.decay_ready, 1)
                if st < KB:
                    if st == 0:
                        eng.wait_ge(s.conv_ready, KB)
                        eng.wait_ge(s.convout_tr, 2)
                    evac(BLK_Q + j, q_t[:, j, :], scale=HEAD ** -0.5).then_inc(s.proj_evac, 1)
                else:
                    if st == KB:
                        eng.wait_ge(s.drive_ready, 1)
                    evac(BLK_GA + j, g_a[:, j, :]).then_inc(s.proj_evac, 1)
                if st == 2:
                    eng.wait_ge(s.var_ready, KB)
                    act(tanh_t[:, :, :], tanh_t[:, :, :], ACT.Sqrt).then_inc(s.mult_ready, 1)
                if st % 2 == 1:
                    attention_exp(st // 2)
                    if st >= 3:
                        eng.wait_ge(s.pt_done, 2 * (st // 2 - 1) + 1)
                        if st >= 5:
                            eng.wait_ge(s.pv_done, st // 2 - 1)
                        act(pt[:, 0, :], bank[6][:, 0:3 * P], ACT.Copy).then_inc(s.pt_evac_a, 1)
                if st >= 4 and st % 2 == 0:
                    jj = (st - 4) // 2
                    eng.wait_ge(s.pv_done, jj + 1)
                    act(m_t[:, KB + jj, 0:2 * P], bank[5][:, 0:2 * P], ACT.Copy).then_inc(s.pv_evac, 1)
                if st == 7:
                    for half in range(2):
                        eng.wait_ge(s.qtok_tr, half + 1)
                        act(q_tok[:, :, half, :], bank[4 + half][0:B_S, :].rearrange("p (g d) -> p g d", g=GROUP),
                            ACT.Copy).then_inc(s.qtok_ready, 1)
                if st == 9:
                    extra_exp(0, p_2[:, 0, :], KEYS2)
                    extra_exp(1, p_2[:, 1, :], KEYS2)
                if st == 10:
                    extra_exp(2, p_d, P)
                if st == 12:
                    eng.wait_ge(s.d_p_tr, 1)
                    act(pt_d[:, :], bank[4][:, 0:P], ACT.Copy).then_inc(s.d_p_ready, 1)
                if st == 13:
                    eng.wait_ge(s.q2_p_tr, 1)
                    act(pt_2[:, 0:2, :].rearrange("p a b -> p (a b)"), bank[5][:, 0:2 * P], ACT.Copy)\
                        .then_inc(s.q2_p_ready, 1)
                    act(pt_2[0:16, 2:4, :].rearrange("p a b -> p (a b)"), bank[5][0:16, 2 * P:4 * P], ACT.Copy)\
                        .then_inc(s.q2_p_ready, 1)
                if st == 14:
                    eng.wait_ge(s.d_pv_done, 1)
                    act(m_t[:, KB:2 * KB, L:T], bank[4][:, 0:KB * B_S].rearrange("p (j b) -> p j b", j=KB), ACT.Copy)\
                        .then_inc(s.d_pv_ready, 1)
                if st == 15:
                    eng.wait_ge(s.q2_pv_done, 1)
                    act(m_t[:, KB:2 * KB, 2 * P:L], bank[4][:, 0:KB * 16].rearrange("p (j q) -> p j q", j=KB), ACT.Copy)\
                        .then_inc(s.q2_pv_ready, 1)
            eng.wait_ge(s.pv_done, KB - 1)
            act(m_t[:, 2 * KB - 2, 0:2 * P], bank[5][:, 0:2 * P], ACT.Copy).then_inc(s.pv_evac, 1)
            eng.wait_ge(s.pt_done, 2 * (KB - 1) + 1)
            act(pt[:, 0, :], bank[6][:, 0:3 * P], ACT.Copy).then_inc(s.pt_evac_a, 1)
            eng.wait_ge(s.pv_done, KB)
            act(m_t[:, 2 * KB - 1, 0:2 * P], bank[5][:, 0:2 * P], ACT.Copy).then_inc(s.pv_evac, 1)
            eng.wait_ge(s.proj_evac, 2 + 4 * KB)
            for half in range(2):
                r = slice(4 * half, 4 * half + 4)
                act(g_a[:, r, :], g_a[:, r, :], ACT.Sigmoid).then_inc(s.ga_sig, 1)
            for half in range(2):
                eng.wait_ge(s.hout_tr, half + 1)
                act(h_out[:, NB * half:NB * (half + 1)], bank[6 + half][0:1 + B_S, :], ACT.Copy).then_inc(s.hout_ready, 1)
            eng.wait_ge(s.hout_ready, 2)
            eng.dma_start(new_h_p[0], h_out[0:1, :]).then_inc(s.hout_stored, 16)
            eng.dma_start(new_h_s[0], h_out[1:1 + B_S, :]).then_inc(s.hout_stored, 16)
            eng.wait_ge(s.wout_used, N_WOUT)
            act(tail_sb[0:TAIL, :], bank[4][64:64 + TAIL, :], ACT.Copy).then_inc(s.tail_moved, 1)
            for t in range(3):
                eng.wait_ge(s.x2_ready, 2 * t + 2)
                if t == 1:
                    eng.wait_ge(s.hout_stored, 32)
                act(h_tok[0:rows(t), t, :], x_tok[0:rows(t), t, :], ACT.Square, accum_out=stat[0:rows(t), t:t + 1])\
                    .then_inc(s.squares, 1)
                eng.wait_ge(s.mean_sq, 1 + t + 1)
                act(stat[0:rows(t), 6 + t:7 + t], stat[0:rows(t), 3 + t:4 + t], ACT.Sqrt).then_inc(s.root, 1)
            for t in range(3):
                n = rows(t)
                for half in range(2):
                    eng.wait_ge(s.h2_tr, 2 * t + half + 1)
                    act(h2_t[:, 4 * half:4 * half + 4, P * t:P * t + n],
                        h2_bank(t, half).rearrange("p (j c) -> p j c", j=4), ACT.Copy).then_inc(s.h2_evac, 1)
            for t in range(3):
                eng.wait_ge(s.negtop, t + 1)
                act(tw[0:rows(t), t, :], top[0:rows(t), t, 0:TOP_K], ACT.Exp, bias=ntop[0:rows(t), t:t + 1],
                    accum_out=tsum[0:rows(t), t:t + 1]).then_inc(s.top_exp, 1)

            def yd_copy(q):
                eng.wait_ge(s.combine_done, 5 * q)
                for c in range(2):
                    if c == 0:
                        eng.wait_ge(s.down_done, q + 1)
                    else:
                        eng.wait_ge(s.ring_used, PAIR_SLOTS * q + PAIR_SLOTS)
                    act(yd[:, NB * c:NB * (c + 1)], bank[4 + c][:, :], ACT.Copy).then_inc(s.yd_ready, 1)

            def sigmoid(q, n):
                eng.wait_ge(s.glu_ready, 4 * q + (n + 1))
                if n < 2:
                    eng.wait_ge(s.y_ready, 4 * q)
                else:
                    eng.wait_ge(s.y_ready, 4 * q + (n - 1))
                act(sig[:, n % 2, :], glu[:, n % 2, :], ACT.Sigmoid, scale=ALPHA).then_inc(s.sig_ready, 1)

            def xe_copy(q, half):
                eng.wait_ge(s.gather_done, 2 * q + (half + 1))
                act(xe[:, 4 * half:4 * half + 4, :].rearrange("p a b -> p (a b)"), bank[6 + half][:, :], ACT.Copy)\
                    .then_inc(s.xt_ready, 1)

            def gwt_copy(q):
                eng.wait_ge(s.gwt_tr, q + 1)
                eng.wait_ge(s.combine_done, 5 * q)
                act(gw_t[:, :], bank[4][:, 0:T], ACT.Copy).then_inc(s.gwt_ready, 1)

            def yt_copy(q):
                for half in range(2):
                    eng.wait_ge(s.ytr_done, 2 * q + (half + 1))
                    act(y_t[:, 4 * half:4 * half + 4, :].rearrange("p a b -> p (a b)"), bank[6 + half][:, :], ACT.Copy)\
                        .then_inc(s.yt_ready, 1)

            def pair(q, gather_next):
                sigmoid(q, 0)
                sigmoid(q, 1)
                if gather_next:
                    xe_copy(q + 1, 0)
                sigmoid(q, 2)
                sigmoid(q, 3)
                if gather_next:
                    xe_copy(q + 1, 1)
                gwt_copy(q)
                yt_copy(q)
                yd_copy(q)

            xe_copy(0, 0)
            xe_copy(0, 1)
            pair(0, True)
            pair(1, True)
            with eng.Fori(1, PAIRS // 2 - 1) as it:
                pair(2 * it, True)
                pair(2 * it + 1, True)
            pair(PAIRS - 2, True)
            pair(PAIRS - 1, False)
            more = eng.value_load(flag[0:1, 0:1], min_val=0, max_val=1)
            with eng.If(more > 0):
                with eng.Fori(PAIRS // 2, PAIRS // 2 * ROUNDS) as it:
                    for u in range(2):
                        xe_copy(2 * it + u, 0)
                        xe_copy(2 * it + u, 1)
                        pair(2 * it + u, False)
            for t in range(3):
                eng.wait_ge(s.moe_done, 1)
                act(h_tok[0:rows(t), t, :], x_tok[0:rows(t), t, :], ACT.Square, accum_out=stat[0:rows(t), t:t + 1])\
                    .then_inc(s.squares, 1)
            for t in range(3):
                eng.wait_ge(s.mean_sq, 4 + t + 1)
                act(stat[0:rows(t), 6 + t:7 + t], stat[0:rows(t), 3 + t:4 + t], ACT.Sqrt).then_inc(s.root, 1)

        @block.tensor
        def _(eng):
            mm = eng.matmul
            eng.wait_ge(s.consts_loaded, 16)
            eng.wait_ge(s.rows_loaded, 16 * 6)
            eng.transpose(bank[7][:, 0:72], vec_in[:, :], ident[0:72, 0:72]).then_inc(s.vec_tr, 1)
            for j in range(KB):
                if j == 7:
                    eng.wait_ge(s.vec_ready, 1)
                for t, (lo, n) in enumerate(TILES):
                    if j == 0:
                        eng.wait_ge(s.xhat_ready, t + 1)
                    tr = eng.transpose(bank[j][:, lo:lo + n], h_tok[0:n, t, P * j:P * (j + 1)], ident[0:n, 0:n])
                tr.then_inc(s.h_tr, 1)

            def scores(j):
                eng.wait_ge(s.proj_evac, BLK_Q + j + 1)
                eng.wait_ge(s.kd_ready, 2)
                eng.wait_ge(s.biased, 2 * j)
                kv = j // 4
                for lo, n in ((0, P), (P, 2 * P)):
                    for p in range(2):
                        h = slice(64 * p, 64 * p + 64)
                        m = mm(bank[2 + p][:, lo:lo + n], q_t[h, j, lo:lo + P], kd[h, kv, 0:n], start=True, stop=True)
                m.then_inc(s.score_done, 1)

            def p_transposes(j):
                eng.wait_ge(s.pt_evac_a, j)
                eng.wait_ge(s.pt_evac_v, j)
                for p in range(2):
                    eng.wait_ge(s.p_scaled, 2 * (2 * j + p) + 2)
                    for c in range(3):
                        tr = eng.transpose(bank[6 + p][:, P * c:P * (c + 1)], probs[:, 2 * (j % 2) + p, P * c:P * (c + 1)],
                                           ident)
                    tr.then_inc(s.pt_done, 1)

            def pv(j):
                eng.wait_ge(s.pt_evac_a, j + 1)
                eng.wait_ge(s.pt_evac_v, j + 1)
                eng.wait_ge(s.pv_evac, j)
                v = slice(64 * (j // 4), 64 * (j // 4) + 64)
                for p in range(2):
                    mm(bank[5][64 * p:64 * p + 64, 0:2 * P], vt[:, 0, v], pt[:, p, 0:2 * P], start=True, stop=False)
                for p in range(2):
                    m = mm(bank[5][64 * p:64 * p + 64, P:2 * P], vt[:, 1, v], pt[:, p, 2 * P:3 * P], start=False, stop=True)
                m.then_inc(s.pv_done, 1)

            def after_kv():
                eng.wait_ge(s.proj_evac, 2)
                for i in range(2):
                    for t, (lo, n) in enumerate(TILES):
                        tr = eng.transpose(bank[6 + i][0:n, P * t:P * (t + 1)], kv_t[:, i, lo:lo + n], ident)
                    tr.then_inc(s.kv_tr, 1)

            def keys_major():
                eng.wait_ge(s.kvtok_ready, 6)
                for kv in range(N_KV):
                    for t, (lo, n) in enumerate(TILES):
                        tr = eng.transpose(bank[6 + kv][:, lo:lo + n], kt4[0:n, t, P * kv:P * (kv + 1)], ident[0:n, 0:n])
                    tr.then_inc(s.kd_tr, 1)

            def states():
                eng.wait_ge(s.kd_ready, 2)
                eng.wait_ge(s.state_loaded, 32)
                for j in range(KB):
                    tr = eng.transpose(bank[6][:, 32 * j:32 * (j + 1)], st_in[:, P * j:P * (j + 1)], ident[0:32, 0:32])
                tr.then_inc(s.state_tr, 1)

            def gates(j):
                eng.wait_ge(s.conv_ready, j + 1)
                eng.wait_ge(s.wgate_loaded, 64)
                for g in range(2):
                    if j:
                        eng.wait_ge(s.gate_evac, 2 * j - 1 + g)
                    mm(bank[4 + g][:, 0:T], wblk[:, g, j, :], xc[:, j, :], start=True, stop=True).then_inc(s.gate_done, 1)

            def conv_rows(half):
                eng.wait_ge(s.state_ready, 2)
                eng.wait_ge(s.xr_ready, KB)
                for i in range(4):
                    tr = eng.transpose(bank[6 + half][0:PAD + B_S, P * i:P * (i + 1)], xr[:, 4 * half + i, L:PAD + T], ident)
                tr.then_inc(s.convout_tr, 1)

            def window_keys(half):
                eng.wait_ge(s.convout_ready, half + 1)
                eng.wait_ge(s.cache_loaded, 32)
                eng.wait_ge(s.newkv_loaded, 64)
                for i in range(4):
                    tr = eng.transpose(bank[6 + half][:, P * i:P * (i + 1)], kc[:, 4 * half + i, :], ident)
                tr.then_inc(s.kc_tr, 1)

            def sample_queries():
                eng.wait_ge(s.proj_evac, BLK_Q + KB)
                eng.wait_ge(s.pv_evac, 2)
                for half in range(2):
                    for i in range(4):
                        tr = eng.transpose(bank[4 + half][0:B_S, P * i:P * (i + 1)], q_t[:, 4 * half + i, L:T], ident)
                    tr.then_inc(s.qtok_tr, 1)

            def sample_heads():
                eng.wait_ge(s.qtok_ready, 2)
                for g in range(GROUP):
                    tr = eng.transpose(bank[4][:, B_S * g:B_S * (g + 1)], q_tok[:, g, :, :].rearrange("b k d -> b (k d)"),
                                       ident[0:B_S, 0:B_S])
                tr.then_inc(s.qd_tr, 1)

            def sample_scores():
                eng.wait_ge(s.qd_ready, 2)
                eng.wait_ge(s.kc_ready, 2)
                qd = qdz.rearrange("p k (g b) -> p k g b", g=GROUP)
                for b in range(B_S):
                    m = mm(bank[4][:, N_HEADS * b:N_HEADS * (b + 1)], kc_t[:, b, :], qd[:, :, :, b], start=True, stop=True)
                m.then_inc(s.dsc_done, 1)

            def last_scores():
                eng.wait_ge(s.q2_ready, 4)
                eng.wait_ge(s.pv_evac, 3)
                for kv in range(N_KV):
                    m = mm(bank[5][:, KEYS2 * kv:KEYS2 * (kv + 1)], q2z[:, kv, :], kd[:, kv, P:L], start=True, stop=True)
                m.then_inc(s.q2_done, 1)

            def sample_rows():
                eng.wait_ge(s.dsc_ready, 1)
                eng.transpose(bank[4][:, 0:P], s_t, ident).then_inc(s.dst_done, 1)

            def sample_p():
                eng.wait_ge(s.x_scaled, 3)
                eng.transpose(bank[4][:, 0:P], p_d, ident).then_inc(s.d_p_tr, 1)

            def last_p():
                eng.wait_ge(s.pv_evac, 5)
                for kv in range(N_KV):
                    eng.transpose(bank[5][:, P * kv:P * (kv + 1)], p_2[:, kv, 0:P], ident)
                for kv in range(N_KV):
                    tr = eng.transpose(bank[5][0:TAIL_P, P * (2 + kv):P * (3 + kv)], p_2[:, kv, P:KEYS2], ident)
                tr.then_inc(s.q2_p_tr, 1)

            def sample_pv():
                eng.wait_ge(s.d_p_ready, 1)
                out = bank[4][:, 0:KB * B_S].rearrange("p (j b) -> p j b", j=KB)
                pr = pt_d.rearrange("p (b k i r) -> p b k i r", b=B_S, k=N_KV, r=2)
                for b in range(B_S):
                    for kv in range(N_KV):
                        for p in range(2):
                            m = mm(out[64 * p:64 * p + 64, 4 * kv:4 * kv + 4, b], vc[:, b, HEAD * kv:HEAD * (kv + 1)],
                                   pr[:, b, kv, :, p], start=True, stop=True)
                m.then_inc(s.d_pv_done, 1)

            def last_pv():
                eng.wait_ge(s.q2_p_ready, 2)
                eng.wait_ge(s.d_pv_ready, 1)
                for kv in range(N_KV):
                    v = slice(HEAD * kv, HEAD * (kv + 1))
                    for p in range(2):
                        o, r = slice(64 * p, 64 * p + 64), slice(64 * p, 64 * p + 64)
                        mm(bank[4][o, 64 * kv:64 * kv + 64], vt[:, 1, v], pt_2[:, kv, r], start=True, stop=False)
                        m = mm(bank[4][o, 64 * kv:64 * kv + 64], vt[0:TAIL_P, 2, v], pt_2[0:TAIL_P, 2 + kv, r],
                               start=False, stop=True)
                m.then_inc(s.q2_pv_done, 1)

            for n in range(2 * N_WIN):
                if n % 2 == 0:
                    g = n // 2
                    eng.wait_ge(ring_full[g % HALF], 16 * (g // HALF + 1))
                    w = ring[:, g % HALF, :].rearrange("p (k c) -> p k c", k=KB)
                if n >= 2:
                    eng.wait_ge(s.proj_evac, n - 1)
                for k in range(KB):
                    if n == 0:
                        eng.wait_ge(s.h_evac_v if k % 2 else s.h_evac_a, k // 2 + 1)
                    m = mm(bank[n % 2][:, 0:T], w[:, k, P * (n % 2):P * (n % 2) + P], h_t[:, k, :],
                           start=(k == 0), stop=(k == KB - 1))
                m.then_inc(s.proj_done, 1)
                {1: after_kv, 3: keys_major, 5: states}.get(n, lambda: None)()
                if BLK_GR <= n < BLK_Q:
                    j = n - BLK_GR
                    gates(j)
                    if j in (3, 4):
                        conv_rows(j - 3)
                    if j in (5, 6):
                        window_keys(j - 5)
                st = n - BLK_Q
                if st < 0:
                    continue
                if st == 3:
                    eng.wait_ge(s.kc_ready, 2)
                if st % 2 == 1:
                    scores(st // 2)
                    if st >= 3:
                        p_transposes(st // 2 - 1)
                elif st >= 4:
                    if st == 8:
                        eng.wait_ge(s.qtok_ready, 2)
                    if st == 10:
                        eng.wait_ge(s.x_biased, 2)
                    if st == 14:
                        eng.wait_ge(s.q2_p_ready, 2)
                    pv((st - 4) // 2)
                if st == 7:
                    sample_queries()
                elif st == 8:
                    sample_heads()
                elif st == 9:
                    sample_scores()
                    last_scores()
                elif st == 10:
                    sample_rows()
                elif st == 12:
                    sample_p()
                elif st == 13:
                    last_p()
                elif st == 14:
                    sample_pv()
                elif st == 15:
                    last_pv()

            eng.wait_ge(s.proj_evac, 2 * N_WIN)
            eng.wait_ge(s.rnn_gated, 1)
            for g in range(N_WOUT):
                n = N_WIN + g
                eng.wait_ge(ring_full[n % HALF], 16 * (n // HALF + 1))
                w = ring[:, n % HALF, :].rearrange("p (j c) -> p j c", j=2)
                if g >= 4:
                    eng.wait_ge(s.attn_gated, 2 * (g - 4) + 2)
                for t in (0, 2, 1):
                    lo, rn = TILES[t]
                    if g == 0 and t == 2:
                        eng.wait_ge(s.q2_pv_ready, 1)
                    if g == 0 and t == 1:
                        eng.wait_ge(s.biased, N_HEADS)
                    for j in range(2):
                        k = 2 * g + j
                        for c in range(2):
                            out = bank[4][64 * c:64 * c + rn, :] if t == 2 else bank[2 * t + c][:, :]
                            m = mm(out, m_t[:, k, lo:lo + rn], w[:, j, NB * c:NB * (c + 1)],
                                   start=(k == 0), stop=(k == 2 * KB - 1))
                m.then_inc(s.wout_used, 1)
                if g == 0:
                    pv(KB - 2)
                    p_transposes(KB - 1)
                if g == 1:
                    pv(KB - 1)
                if g == 2:
                    eng.wait_ge(s.pt_evac_a, KB)
                    eng.wait_ge(s.pt_evac_v, KB)
                    for half in range(2):
                        for i in range(4):
                            tr = eng.transpose(bank[6 + half][0:1 + B_S, P * i:P * (i + 1)],
                                               xc[:, 4 * half + i, L - 1:T], ident)
                        tr.then_inc(s.hout_tr, 1)

            eng.wait_ge(s.pv_evac, KB)
            eng.wait_ge(s.hout_ready, 2)
            for t, (lo, n) in enumerate(TILES):
                eng.wait_ge(s.h2_ready, t + 1)
                for half in range(2):
                    for i in range(4):
                        j = 4 * half + i
                        tr = eng.transpose(h2_bank(t, half)[:, n * i:n * (i + 1)], h_tok[0:n, t, P * j:P * (j + 1)],
                                           ident[0:n, 0:n])
                    tr.then_inc(s.h2_tr, 1)
            eng.wait_ge(s.router_loaded, 32)
            for t, (lo, n) in enumerate(TILES):
                eng.wait_ge(s.h2_evac, 2 * t + 2)
                for k in range(KB):
                    m = mm(lg_bank[t][0:n, 0:E_N], h2_t[:, k, lo:lo + n], wr[:, k, :],
                           start=(k == 0), stop=(k == KB - 1))
                m.then_inc(s.logits_done, 1)
            eng.wait_ge(s.selb_ready, 1)
            eng.wait_ge(s.cast_ready, 2)
            eng.wait_ge(s.zeroed, 1)
            for t in range(3):
                for t2 in range(t + 1):
                    mm(bank[3][:, E_N * t:E_N * (t + 1)], tri[:, :] if t2 == t else ones[:, :], selb[:, t2, :],
                       start=(t2 == 0), stop=(t2 == t))
            for t in range(3):
                m = mm(bank[3][0:1, 3 * E_N:4 * E_N], ones[:, 0:1], selb[:, t, :], start=(t == 0), stop=(t == 2))
            m.then_inc(s.rank_done, 1)

            def gather(q, u, combined):
                eng.wait_ge(s.gather_oh, q + 1)
                if combined is not None:
                    eng.wait_ge(s.added, 5 * combined)
                for half in range(2):
                    for i in range(4):
                        j = 4 * half + i
                        for t, (lo, n) in enumerate(TILES):
                            m = mm(bank[6 + half][:, P * i:P * (i + 1)], h_tok[0:n, t, P * j:P * (j + 1)],
                                   g_oh[0:n, t, :], start=(t == 0), stop=(t == 2))
                    m.then_inc(s.gather_done, 1)

            def combine(q, unit):
                if unit == 0:
                    eng.wait_ge(s.gwt_ready, q + 1)
                    eng.wait_ge(s.yd_ready, 2 * q + 2)
                elif unit >= 2:
                    eng.wait_ge(s.added, 5 * q + (unit - 1))
                b = bank[6 + unit % 2]
                if unit < 4:
                    lo, c = P * (unit // 2), unit % 2
                    m = mm(b[:, :], gw_t[:, lo:lo + P], yd[:, NB * c:NB * (c + 1)], start=True, stop=True)
                else:
                    for c in range(2):
                        m = mm(b[64 * c:64 * c + TAIL, :], gw_t[:, 2 * P:T], yd[:, NB * c:NB * (c + 1)],
                               start=True, stop=True)
                m.then_inc(s.combine_done, 1)

            def full(u, i, it):
                slot, turn, before = ring_place(PAIR_SLOTS * u + i)
                eng.wait_ge(ring_full[slot], 48 * it + 16 * (turn + before + 1))
                return ring[:, slot, :]

            def pair(q, u, it, pq, pipelined, first=False, last=False):
                chosen = pick[:, bass.ds(2 * pq, 2), :].rearrange("p e c -> p (e c)")
                eng.wait_ge(s.y_ready, 4 * q)
                eng.wait_ge(s.xt_ready, 2 * q + 2)
                for n in range(4):
                    mm(bank[n][:, :], chosen, bias_parts[:, NB * n:NB * (n + 1)], start=True, stop=False,
                       skip_group_check=True)
                for k in range(KB):
                    w = [full(u, 2 * k + e, it) for e in range(2)]
                    for n in range(4):
                        for e in range(2):
                            m = mm(bank[n][64 * e:64 * e + 64, :], xe[:, k, 64 * e:64 * e + 64],
                                   w[e][:, NB * n:NB * (n + 1)], start=False, stop=(k == KB - 1), skip_group_check=True)
                            if n == 3:
                                m.then_inc(s.ring_used, 1)
                            elif k == KB - 1 and e == 1:
                                m.then_inc(s.up_done, 1)
                    if pipelined and not first and 1 <= k <= 5:
                        combine(q - 1, k - 1)
                if pipelined and not last:
                    gather(q + 1, None, None if first else q)
                eng.wait_ge(s.weight_oh, q + 1)
                eng.wait_ge(s.yd_ready, 2 * q)
                for t, (lo, n) in enumerate(TILES):
                    tr = eng.transpose(bank[4][:, lo:lo + n], gw[u][0:n, t, :], ident[0:n, 0:n])
                tr.then_inc(s.gwt_tr, 1)
                if pipelined and not last:
                    eng.wait_ge(s.xt_ready, 2 * q + 4)
                elif pipelined:
                    eng.wait_ge(s.added, 5 * q)
                for half in range(2):
                    eng.wait_ge(s.y_ready, 4 * q + (2 * half + 2))
                    for i in range(4):
                        tr = eng.transpose(bank[6 + half][:, P * i:P * (i + 1)],
                                           y_e[:, P * (4 * half + i):P * (4 * half + i + 1)], ident)
                    tr.then_inc(s.ytr_done, 1)
                eng.wait_ge(s.gwt_ready, q + 1)
                for c in range(2):
                    mm(bank[4 + c][:, :], chosen, bias_parts[:, NB * (4 + c):NB * (5 + c)], start=True, stop=False,
                       skip_group_check=True)
                for fp in range(KB // 2):
                    if fp % 2 == 0:
                        eng.wait_ge(s.yt_ready, 2 * q + (fp // 2 + 1))
                    w = [full(u, UP_SLOTS + 2 * fp + e, it) for e in range(2)]
                    for j in range(2):
                        for c in range(2):
                            for e in range(2):
                                f = 2 * fp + j
                                m = mm(bank[4 + c][64 * e:64 * e + 64, :], y_t[:, f, 64 * e:64 * e + 64],
                                       w[e][:, D * j + NB * c:D * j + NB * (c + 1)], start=False, stop=(f == KB - 1),
                                       skip_group_check=True)
                                if j == 1 and c == 1:
                                    m.then_inc(s.ring_used, 1)
                                elif f == KB - 1 and e == 1:
                                    m.then_inc(s.down_done, 1)

            gather(0, 0, None)
            pair(0, 0, 0, 0, True, first=True)
            pair(1, 1, 0, 1, True)
            with eng.Fori(1, PAIRS // 2 - 1) as it:
                for u in range(2):
                    pair(2 * it + u, u, it, 2 * it + u, True)
            pair(PAIRS - 2, 0, PAIRS // 2 - 1, PAIRS - 2, True)
            pair(PAIRS - 1, 1, PAIRS // 2 - 1, PAIRS - 1, True, last=True)
            for unit in range(5):
                combine(PAIRS - 1, unit)
            eng.wait_ge(s.flag_ready, 1)
            more = eng.value_load(flag[0:1, 0:1], min_val=0, max_val=1)
            with eng.If(more > 0):
                with eng.Fori(1, ROUNDS) as rnd:
                    with eng.Fori(0, PAIRS // 2) as i2:
                        for u in range(2):
                            it = PAIRS // 2 * rnd + i2
                            q = 2 * it + u
                            gather(q, u, q)
                            pair(q, u, it, 2 * i2 + u, False)
                            for unit in range(5):
                                combine(q, unit)

        @block.vector
        def _(eng):
            eng.memset(stat[:, :], 1.0).then_inc(s.sums_zeroed, 1)
            eng.wait_ge(s.consts_loaded, 16)
            for t in range(3):
                eng.wait_ge(s.squares, t + 1)
            eng.tensor_scalar(stat[:, 3:6], stat[:, 0:3], 1.0 / D, EPS, ALU.mult, ALU.add).then_inc(s.mean_sq, 1)
            eng.wait_ge(s.root, 1)
            eng.reciprocal(stat[:, 9:12], stat[:, 6:9]).then_inc(s.rstd_ready, 1)
            eng.wait_ge(s.rstd_ready, 1)
            for t in range(3):
                n = rows(t)
                eng.tensor_scalar(h_tok[0:n, t, :], x_tok[0:n, t, :], stat[0:n, 9 + t:10 + t], None, ALU.mult)\
                   .then_inc(s.xhat_ready, 1)
            eng.wait_ge(s.vec_tr, 1)
            eng.tensor_copy(vec[:, :], bank[7][:, 0:72]).then_inc(s.vec_ready, 1)
            eng.wait_ge(s.vec_ready, 1)
            for j in range(1, KB, 2):
                eng.wait_ge(s.h_tr, j + 1)
                eng.tensor_scalar(h_t[:, j, :], bank[j][:, 0:T], vec[:, NRM + j:NRM + j + 1], None, ALU.mult)\
                   .then_inc(s.h_evac_v, 1)
            def stepper(sem):
                done = 0

                def step(ins):
                    nonlocal done
                    ins.then_inc(sem, 1)
                    done += 1
                    eng.wait_ge(sem, done)
                return step

            lam = vec[:, LAM:LAM + KB]
            v = [sm[:, 16 + 8 * i:24 + 8 * i] for i in range(5)]
            step = stepper(s.sp_step)
            step(eng.tensor_scalar(v[0], lam, -1.0, None, ALU.mult))
            step(eng.tensor_tensor(v[1], v[0], lam, ALU.min))
            eng.tensor_copy(sm[:, 0:8], v[1]).then_inc(s.sp_in, 1)
            eng.wait_ge(s.sp_exp, 1)
            e = sm[:, 8:16]
            step(eng.tensor_scalar(v[1], e, 2.0, None, ALU.add))
            step(eng.reciprocal(v[1], v[1]))
            step(eng.tensor_tensor(v[1], v[1], e, ALU.mult))
            step(eng.tensor_tensor(v[2], v[1], v[1], ALU.mult))
            step(eng.tensor_scalar(v[3], v[2], 1.0 / 17, None, ALU.mult))
            for k in range(7, 0, -1):
                step(eng.scalar_tensor_tensor(out=v[3], in0=v[3], scalar=1.0 / (2 * k + 1), in1=v[2],
                                              op0=ALU.add, op1=ALU.mult))
            step(eng.scalar_tensor_tensor(out=v[3], in0=v[3], scalar=1.0, in1=v[1], op0=ALU.add, op1=ALU.mult))
            step(eng.tensor_scalar(v[0], v[0], 0.0, LRU_C, ALU.max, ALU.mult))
            step(eng.scalar_tensor_tensor(out=decay[:, 0:KB], in0=v[3], scalar=2 * LRU_C, in1=v[0],
                                          op0=ALU.mult, op1=ALU.add))
            step(eng.tensor_scalar(decay[:, KB:2 * KB], decay[:, 0:KB], -1.0, None, ALU.mult))
            eng.wait_ge(s.masks_loaded, 16)
            eng.wait_ge(s.sinks_loaded, 16)
            eng.tensor_copy(tri[:, :], msk(C_TRI, P)).then_inc(s.cast_ready, 1)
            eng.tensor_copy(pick[:, :, :], masks[0:3 * E_N, C_SEL - C_KEEP:C_SEL - C_KEEP + E_N].unsqueeze(2)
                            .to_broadcast([3 * E_N, E_N, CAP])).then_inc(s.cast_ready, 1)
            for n, c in enumerate((C_OH2, C_OH2 + N_HEADS, C_OHD)):
                eng.tensor_tensor(msk(c, N_HEADS), msk(c, N_HEADS), sinks[:, :], ALU.mult).then_inc(s.sinkcol_step, 1)
                eng.wait_ge(s.sinkcol_step, 2 * n + 1)
                eng.tensor_reduce(snk[:, n:n + 1], msk(c, N_HEADS), AX.X, ALU.add).then_inc(s.sinkcol_step, 1)
            for i in range(2):
                eng.wait_ge(s.kv_tr, i + 1)
                src = bank[6 + i][:, 0:3 * P].rearrange("p (t k d) -> p t k d", t=3, k=N_KV)
                for dup in range(2 - i):
                    dst = (kt4.rearrange("p t (k r d) -> p t k r d", k=N_KV, r=2)[:, :, :, dup, :] if i == 0
                           else vt.rearrange("p t (k d) -> p t k d", k=N_KV))
                    eng.tensor_copy(dst[:, 0:2], src[:, 0:2]).then_inc(s.kvtok_ready, 1)
                    eng.tensor_copy(dst[0:TAIL, 2], src[0:TAIL, 2]).then_inc(s.kvtok_ready, 1)
            eng.wait_ge(s.state_tr, 1)
            st = bank[6][:, 0:32 * KB].rearrange("p (j r) -> p j r", j=KB)
            eng.tensor_copy(sdec[:, :, :], st[:, :, 0:PAD * B_S]).then_inc(s.state_ready, 1)
            eng.tensor_copy(h0[:, :, :], st[:, :, PAD * B_S:32]).then_inc(s.state_ready, 1)
            eng.wait_ge(s.state_ready, 2)
            n = 0
            for j in range(KB):
                eng.wait_ge(s.proj_evac, BLK_XR + j + 1)
                old = sdec[:, j, :].rearrange("p (b r) -> p b r", r=PAD)
                for i in range(PAD):
                    w = vec[:, CW + KB * i + j:CW + KB * i + j + 1]
                    if i:
                        eng.wait_ge(s.conv_step, n)
                    eng.scalar_tensor_tensor(out=xc[:, j, 0:L], in0=xr[:, j, i:i + L], scalar=w, in1=xc[:, j, 0:L],
                                             op0=ALU.mult, op1=ALU.add).then_inc(s.conv_step, 1)
                    ins = eng.scalar_tensor_tensor(out=xc[:, j, L:T], in0=old[:, :, i], scalar=w, in1=xc[:, j, L:T],
                                                   op0=ALU.mult, op1=ALU.add)
                    if i < PAD - 1:
                        ins.then_inc(s.conv_step, 1)
                        n += 2
                    else:
                        ins.then_inc(s.conv_ready, 1)
                        n += 1
            for half in range(2):
                eng.wait_ge(s.convout_tr, half + 1)
                eng.tensor_copy(conv_out[:, NB * half:NB * (half + 1)], bank[6 + half][0:PAD + B_S, :])\
                   .then_inc(s.convout_ready, 1)

            def attention_bias(j):
                eng.wait_ge(s.score_done, j + 1)
                if j >= 2:
                    eng.wait_ge(s.pt_done, 2 * (j - 1))
                for p in range(2):
                    h = 2 * j + p
                    buf, col = probs[:, 2 * (j % 2) + p, :], 16 * (j % 2) + 8 * p
                    eng.scalar_tensor_tensor(out=buf, in0=msk(C_DQ, 3 * P), scalar=SLOPES[h], in1=bank[2 + p][:, 0:3 * P],
                                             op0=ALU.mult, op1=ALU.add).then_inc(s.biased, 1)
                for p in range(2):
                    h = 2 * j + p
                    buf, col = probs[:, 2 * (j % 2) + p, :], 16 * (j % 2) + 8 * p
                    eng.wait_ge(s.biased, h + 1)
                    eng.tensor_reduce(sm[:, col + 2:col + 3], buf[:, 0:P], AX.X, ALU.max).then_inc(s.rowmax, 1)
                    eng.tensor_reduce(sm[:, col + 3:col + 4], buf[:, P:3 * P], AX.X, ALU.max).then_inc(s.rowmax, 1)
                for p in range(2):
                    h = 2 * j + p
                    col = 16 * (j % 2) + 8 * p
                    eng.wait_ge(s.rowmax, 2 * h + 2)
                    eng.tensor_scalar(sm[:, col + 2:col + 4], sm[:, col + 2:col + 4], sinks[:, h:h + 1], -1.0,
                                      ALU.max, ALU.mult).then_inc(s.negmax, 1)

            def attention_sum(j):
                for p in range(2):
                    h = 2 * j + p
                    col = 16 * (j % 2) + 8 * p
                    eng.wait_ge(s.exp_done, 2 * h + 2)
                    eng.wait_ge(s.sink_exp, h + 1)
                    eng.tensor_tensor(sm[:, col + 4:col + 6], sm[:, col + 4:col + 6], sm[:, col:col + 2], ALU.add)\
                       .then_inc(s.denom, 1)
                    eng.wait_ge(s.denom, h + 1)
                    eng.reciprocal(sm[:, col + 6:col + 8], sm[:, col + 4:col + 6]).then_inc(s.rden, 1)

            def pt_copy(j):
                eng.wait_ge(s.pt_done, 2 * j + 2)
                eng.wait_ge(s.pv_done, j)
                eng.tensor_copy(pt[:, 1, :], bank[7][:, 0:3 * P]).then_inc(s.pt_evac_v, 1)

            def extra_bias(n, buf, width, dist, slope, scores):
                col = 32 + 6 * n
                eng.scalar_tensor_tensor(out=buf, in0=dist, scalar=slope, in1=scores, op0=ALU.mult, op1=ALU.add)\
                   .then_inc(s.x_biased, 1)
                eng.wait_ge(s.x_biased, n + 1)
                eng.tensor_reduce(sm[:, col + 1:col + 2], buf, AX.X, ALU.max).then_inc(s.x_step, 1)
                eng.wait_ge(s.x_step, (1, 2, 7)[n])
                eng.tensor_scalar(sm[:, col + 1:col + 2], sm[:, col + 1:col + 2], snk[:, n:n + 1], -1.0,
                                  ALU.max, ALU.mult).then_inc(s.x_negmax, 1)

            def extra_sum(n, buf):
                col = 32 + 6 * n
                eng.wait_ge(s.x_exp, n + 1)
                eng.wait_ge(s.x_sink_exp, n + 1)
                eng.tensor_tensor(sm[:, col + 2:col + 3], sm[:, col + 2:col + 3], sm[:, col:col + 1], ALU.add)\
                   .then_inc(s.x_step, 1)
                eng.wait_ge(s.x_step, (3, 5, 8)[n])
                eng.reciprocal(sm[:, col + 3:col + 4], sm[:, col + 2:col + 3]).then_inc(s.x_step, 1)
                eng.wait_ge(s.x_step, (4, 6, 9)[n])
                eng.tensor_scalar(buf, buf, sm[:, col + 3:col + 4], None, ALU.mult).then_inc(s.x_scaled, 1)

            for j in range(KB):
                eng.wait_ge(s.decay_ready, j + 1)
                if j:
                    eng.wait_ge(s.var_ready, j)
                eng.tensor_tensor(lru_tmp, a_t[:, j, :], a_t[:, j, :], ALU.mult).then_inc(s.lru_step, 1)
                eng.wait_ge(s.lru_step, j + 1)
                eng.scalar_tensor_tensor(out=tanh_t[:, j, :], in0=lru_tmp, scalar=1.0, in1=tanh_t[:, j, :],
                                         op0=ALU.add, op1=ALU.mult).then_inc(s.var_ready, 1)
            eng.wait_ge(s.convout_stored, 32)
            attention_bias(0)
            attention_sum(0)
            eng.wait_ge(s.mult_ready, 1)
            eng.wait_ge(s.ix_ready, KB)
            eng.memset(tanh_t[:, :, 0:1], 1.0).then_inc(s.lru_step, 1)
            eng.wait_ge(s.lru_step, KB + 1)
            eng.tensor_tensor(b_t[:, :, :], b_t[:, :, :], tanh_t[:, :, :], ALU.mult).then_inc(s.drive_ready, 1)
            eng.wait_ge(s.drive_ready, 1)
            attention_bias(1)
            pt_copy(0)
            attention_sum(1)
            for j in range(KB):
                eng.tensor_tensor_scan(xc[:, j, 0:L], a_t[:, j, 0:L], b_t[:, j, 0:L], 0.0, ALU.mult, ALU.add)\
                   .then_inc(s.lru_step, 1)
            eng.tensor_tensor(h0[:, :, :], h0[:, :, :], a_t[:, :, L:T], ALU.mult).then_inc(s.lru_step, 1)
            eng.wait_ge(s.lru_step, 2 * KB + 2)
            eng.tensor_tensor(xc[:, :, L:T], h0[:, :, :], b_t[:, :, L:T], ALU.add).then_inc(s.lru_step, 1)
            eng.wait_ge(s.lru_step, 2 * KB + 3)
            eng.wait_ge(s.bias_step, 9)
            eng.tensor_tensor(m_t[:, 0:KB, :], g_r[:, :, :], xc[:, :, :], ALU.mult).then_inc(s.rnn_gated, 1)
            for j in range(2, KB):
                attention_bias(j)
                pt_copy(j - 1)
                if j == 3:
                    eng.wait_ge(s.proj_evac, BLK_Q + KB)
                    eng.wait_ge(s.zeroed, 4)
                    for kv in range(N_KV):
                        for p in range(2):
                            eng.tensor_copy(q2z[64 * p:64 * p + 64, kv, 64 * p:64 * p + 64]
                                            .rearrange("p (i q) -> p i q", i=4),
                                            q_t[64 * p:64 * p + 64, 4 * kv:4 * kv + 4, 2 * P:L]).then_inc(s.q2_ready, 1)
                    attention_sum(j)
                    eng.wait_ge(s.qd_tr, 1)
                    for kv in range(N_KV):
                        h = slice(64 * kv, 64 * kv + 64)
                        eng.tensor_copy(qdz[h, kv, :], bank[4][h, 0:GROUP * B_S]).then_inc(s.qd_ready, 1)
                elif j == 4:
                    attention_sum(j)
                    eng.wait_ge(s.dsc_done, 1)
                    eng.tensor_copy(s_t, bank[4][:, 0:P]).then_inc(s.dsc_ready, 1)
                    eng.wait_ge(s.q2_done, 1)
                    for kv in range(N_KV):
                        extra_bias(kv, p_2[:, kv, :], KEYS2, msk(C_D2, KEYS2), msk(C_SL2 + kv, 1),
                                   bank[5][:, KEYS2 * kv:KEYS2 * (kv + 1)])
                    for kv in range(N_KV):
                        extra_sum(kv, p_2[:, kv, :])
                    eng.wait_ge(s.dst_done, 1)
                    extra_bias(2, p_d, P, msk(C_DD, P), msk(C_SLD, 1), bank[4][:, 0:P])
                elif j == 5:
                    attention_sum(j)
                    extra_sum(2, p_d)
                else:
                    attention_sum(j)
            pt_copy(KB - 1)
            eng.wait_ge(s.d_pv_ready, 1)
            eng.wait_ge(s.q2_pv_ready, 1)
            for j in range(KB):
                eng.wait_ge(s.pv_evac, j + 1)
                eng.wait_ge(s.ga_sig, j // 4 + 1)
                eng.tensor_tensor(m_t[:, KB + j, :], m_t[:, KB + j, :], g_a[:, j, :], ALU.mult).then_inc(s.attn_gated, 1)

            eng.wait_ge(s.window_stored, 32)
            router_step = stepper(s.router_step)
            router_step(eng.memset(topf[:, :, :], -1.0))
            router_step(eng.memset(tw[:, :, :], 0.0))
            eng.wait_ge(s.wout_used, N_WOUT)
            for t in range(3):
                n = rows(t)
                for c in range(2):
                    x = x_tok[0:n, t, NB * c:NB * (c + 1)]
                    if t == 2 and c == 1:
                        eng.wait_ge(s.tail_moved, 1)
                    src = bank[2 * t + c][0:n, :] if t < 2 else (bank[4][0:n, :], tail_sb[0:n, :])[c]
                    eng.tensor_tensor(x, x, src, ALU.add).then_inc(s.x2_ready, 1)
            eng.wait_ge(s.norm_loaded, 16)
            eng.wait_ge(s.x2_ready, 6)
            for t in range(3):
                n = rows(t)
                eng.wait_ge(s.squares, 3 + t + 1)
                eng.tensor_scalar(stat[0:n, 3 + t:4 + t], stat[0:n, t:t + 1], 1.0 / D, EPS, ALU.mult, ALU.add)\
                   .then_inc(s.mean_sq, 1)
                eng.wait_ge(s.root, 1 + t + 1)
                eng.reciprocal(stat[0:n, 9 + t:10 + t], stat[0:n, 6 + t:7 + t]).then_inc(s.rstd_ready, 1)
                eng.wait_ge(s.rstd_ready, 1 + t + 1)
                eng.scalar_tensor_tensor(out=h_tok[0:n, t, :], in0=x_tok[0:n, t, :], scalar=stat[0:n, 9 + t:10 + t],
                                         in1=norm_b[0:n, :], op0=ALU.mult, op1=ALU.mult).then_inc(s.h2_ready, 1)
            eng.wait_ge(s.router_loaded, 32)
            for t in range(3):
                n = rows(t)
                eng.wait_ge(s.logits_done, t + 1)
                router_step(eng.tensor_tensor(lg[0:n, t, :], lg_bank[t][0:n, 0:E_N], br[0:n, :], ALU.add))
                router_step(eng.max(top[0:n, t, :], lg[0:n, t, :]))
                eng.tensor_scalar(ntop[0:n, t:t + 1], top[0:n, t, 0:1], -1.0, None, ALU.mult).then_inc(s.negtop, 1)
                router_step(eng.max_index(topi[0:n, t, :], top[0:n, t, :], lg[0:n, t, :]))
                router_step(eng.tensor_copy(topf[0:n, t, :], topi[0:n, t, 0:TOP_K]))
            flat = [P, 3 * TOP_K, E_N]
            router_step(eng.tensor_tensor(eq[:, :, :], iota[:, 0:E_N].unsqueeze(1).to_broadcast(flat),
                                          topf.rearrange("p t k -> p (t k)").unsqueeze(2).to_broadcast(flat),
                                          ALU.is_equal))
            router_step(eng.tensor_reduce(sel[:, :, :], eq.rearrange("p (t k) e -> p t e k", t=3), AX.X, ALU.add))
            eng.tensor_copy(selb[:, :, :], sel[:, :, :]).then_inc(s.selb_ready, 1)
            for t in range(3):
                n = rows(t)
                eng.wait_ge(s.top_exp, t + 1)
                router_step(eng.reciprocal(tsum[0:n, t:t + 1], tsum[0:n, t:t + 1]))
                router_step(eng.tensor_scalar(tw[0:n, t, :], tw[0:n, t, :], tsum[0:n, t:t + 1], None, ALU.mult))
            router_step(eng.tensor_tensor(eqw[:, :, :], eq[:, :, :],
                                          tw.rearrange("p t k -> p (t k)").unsqueeze(2).to_broadcast(flat), ALU.mult))
            router_step(eng.tensor_reduce(wts[:, :, :], eqw.rearrange("p (t k) e -> p t e k", t=3), AX.X, ALU.add))
            eng.wait_ge(s.rank_done, 1)
            router_step(eng.scalar_tensor_tensor(out=rank_m[:, :, :], in0=bank[3][:, 0:3 * E_N]
                                                 .rearrange("p (t e) -> p t e", t=3), scalar=1.0, in1=sel[:, :, :],
                                                 op0=ALU.add, op1=ALU.mult))
            router_step(eng.tensor_scalar(rank_m[:, :, :], rank_m[:, :, :], -1.0, None, ALU.add))
            router_step(eng.tensor_reduce(cnt[0:1, 0, 0:1], bank[3][0:1, 3 * E_N:4 * E_N], AX.X, ALU.max))
            eng.tensor_scalar(flag[:, :], cnt[0:1, 0, 0:1], float(CAP), None, ALU.is_gt).then_inc(s.flag_ready, 1)

            def one_hots(q, u, pq, slots, reused):
                shape = [P, 3, 2, CAP]
                view = "p t (e c) -> p t e c"
                rk = rank_m[:, :, bass.ds(2 * pq, 2)].unsqueeze(3).to_broadcast(shape)
                wt = wts[:, :, bass.ds(2 * pq, 2)].unsqueeze(3).to_broadcast(shape)
                eng.wait_ge(s.gather_done, 2 * q)
                eng.wait_ge(s.weight_oh, q)
                eng.tensor_tensor(g_oh.rearrange(view, e=2), slots.unsqueeze(1).unsqueeze(1).to_broadcast(shape), rk,
                                  ALU.is_equal).then_inc(s.gather_oh, 1)
                eng.wait_ge(s.gather_oh, q + 1)
                if reused:
                    eng.wait_ge(s.gwt_tr, q - 1)
                eng.tensor_tensor(gw[u].rearrange(view, e=2), g_oh.rearrange(view, e=2), wt, ALU.mult)\
                   .then_inc(s.weight_oh, 1)

            def add(q):
                eng.wait_ge(s.added, 5 * q)
                eng.wait_ge(s.tail_added, q)
                for unit in range(5):
                    eng.wait_ge(s.combine_done, 5 * q + (unit + 1))
                    b = bank[6 + unit % 2]
                    if unit < 4:
                        x = x_tok[:, unit // 2, NB * (unit % 2):NB * (unit % 2 + 1)]
                        eng.tensor_tensor(x, x, b[:, :], ALU.add).then_inc(s.added, 1)
                    else:
                        eng.tensor_copy(tail_sb[0:TAIL, :], b[64:64 + TAIL, :]).then_inc(s.tail_copied, 1)
                        x = x_tok[0:TAIL, 2, 0:NB]
                        eng.tensor_tensor(x, x, b[0:TAIL, :], ALU.add).then_inc(s.added, 1)
                        eng.wait_ge(s.tail_copied, q + 1)
                        x = x_tok[0:TAIL, 2, NB:D]
                        eng.tensor_tensor(x, x, tail_sb[0:TAIL, :], ALU.add).then_inc(s.tail_added, 1)

            def gating(q):
                def clamp(n):
                    if n < 3:
                        eng.wait_ge(s.up_done, 3 * q + (n + 1))
                    else:
                        eng.wait_ge(s.ring_used, PAIR_SLOTS * q + UP_SLOTS)
                    eng.wait_ge(s.y_ready, 4 * q + (n - 1 if n > 1 else 0))
                    z = bank[n][:, :].rearrange("p (f two) -> p f two", two=2)
                    eng.tensor_scalar(glu[:, n % 2, :], z[:, :, 0], LIMIT, None, ALU.min).then_inc(s.glu_ready, 1)
                    eng.tensor_scalar(lin[:, n % 2, :], z[:, :, 1], LIMIT, -LIMIT, ALU.min, ALU.max)\
                       .then_inc(s.lin_ready, 1)
                    eng.wait_ge(s.lin_ready, 4 * q + (n + 1))
                    eng.scalar_tensor_tensor(out=lin[:, n % 2, :], in0=lin[:, n % 2, :], scalar=1.0, in1=glu[:, n % 2, :],
                                             op0=ALU.add, op1=ALU.mult).then_inc(s.gated_ready, 1)

                def finish(n):
                    eng.wait_ge(s.gated_ready, 4 * q + (n + 1))
                    eng.wait_ge(s.sig_ready, 4 * q + (n + 1))
                    if n == 0:
                        eng.wait_ge(s.ytr_done, 2 * q)
                    eng.tensor_tensor(y_e[:, COLS * n:COLS * (n + 1)], lin[:, n % 2, :], sig[:, n % 2, :], ALU.mult)\
                       .then_inc(s.y_ready, 1)

                clamp(0)
                for n in range(1, 4):
                    clamp(n)
                    finish(n - 1)
                finish(3)

            first = iota[:, 0:CAP]
            one_hots(0, 0, 0, first, False)
            one_hots(1, 1, 1, first, False)
            gating(0)
            one_hots(2, 0, 2, first, True)
            add(0)
            gating(1)
            with eng.Fori(1, PAIRS // 2 - 1) as it:
                for u in range(2):
                    q = 2 * it + u
                    one_hots(q + 1, 1 - u, q + 1, first, True)
                    add(q - 1)
                    gating(q)
            one_hots(PAIRS - 1, 1, PAIRS - 1, first, True)
            add(PAIRS - 3)
            gating(PAIRS - 2)
            add(PAIRS - 2)
            gating(PAIRS - 1)
            add(PAIRS - 1)
            more = eng.value_load(flag[0:1, 0:1], min_val=0, max_val=1)
            with eng.If(more > 0):
                with eng.Fori(1, ROUNDS) as rnd:
                    with eng.Fori(0, PAIRS // 2) as i2:
                        for u in range(2):
                            q = PAIRS * rnd + 2 * i2 + u
                            one_hots(q, u, 2 * i2 + u, iota[:, bass.ds(CAP * rnd, CAP)], True)
                            gating(q)
                            add(q)
            eng.memset(stat[:, :], 1.0).then_inc(s.moe_done, 1)
            eng.wait_ge(s.fnorm_loaded, 16)
            for t in range(3):
                n = rows(t)
                eng.wait_ge(s.squares, 6 + t + 1)
                eng.tensor_scalar(stat[0:n, 3 + t:4 + t], stat[0:n, t:t + 1], 1.0 / D, EPS, ALU.mult, ALU.add)\
                   .then_inc(s.mean_sq, 1)
            for t in range(3):
                n = rows(t)
                eng.wait_ge(s.root, 4 + t + 1)
                eng.reciprocal(stat[0:n, 9 + t:10 + t], stat[0:n, 6 + t:7 + t]).then_inc(s.rstd_ready, 1)
                eng.wait_ge(s.rstd_ready, 4 + t + 1)
                eng.scalar_tensor_tensor(out=h_tok[0:n, t, :], in0=x_tok[0:n, t, :], scalar=stat[0:n, 9 + t:10 + t],
                                         in1=norm_b[0:n, :], op0=ALU.mult, op1=ALU.mult).then_inc(s.y_final, 1)


INPUTS = ["x_prompt", "x_sample", "cache_k", "cache_v", "state_conv", "state_h", "meta_tokens", "norm_mix", "w_in",
          "conv_w", "conv_b", "w_rg", "b_rg", "w_ig", "b_ig", "lru_lambda", "attn_sinks", "w_out", "norm_ffn",
          "w_router", "b_router", "w_up", "b_up", "w_down", "b_down", "norm_final"]
OUTPUTS = [("y_prompt", (1, SEQ, D)), ("y_sample", (B_S, 1, D)),
           ("new_k_prompt", (1, 1, WINDOW, N_KV, HEAD)), ("new_v_prompt", (1, 1, WINDOW, N_KV, HEAD)),
           ("new_conv_prompt", (1, 1, PAD, D)), ("new_h_prompt", (1, 1, D)),
           ("new_k_sample", (1, B_S, WINDOW, N_KV, HEAD)), ("new_v_sample", (1, B_S, WINDOW, N_KV, HEAD)),
           ("new_conv_sample", (1, B_S, PAD, D)), ("new_h_sample", (1, B_S, D))]


def kernel(**inputs):
    import concourse.bacc as bacc
    from concourse.bass_utils import run_bass_kernel_spmd

    nc = bacc.Bacc("TRN2", target_bir_lowering=False, num_devices=1, dynamic_dma_scratch_size=64)
    arrays = {"in_constants": shape_constants()}
    for name in INPUTS:
        arrays["in_" + name] = np.ascontiguousarray(inputs[name])
    args = [nc.dram_tensor(n, a.shape, mybir.dt.from_np(a.dtype), kind="ExternalInput").ap() for n, a in arrays.items()]
    args += [nc.dram_tensor("out_" + n, shape, F32, kind="ExternalOutput").ap() for n, shape in OUTPUTS]
    program(nc, *args)
    result = run_bass_kernel_spmd(nc, [arrays], core_ids=[0]).results[0]
    return tuple(result["out_" + n] for n, _ in OUTPUTS)
```

```python
from collections import namedtuple
from contextlib import ExitStack

import numpy as np

import concourse.bass as bass
from concourse import mybir

F32 = mybir.dt.float32
BF16 = mybir.dt.bfloat16
I32 = mybir.dt.int32
U32 = mybir.dt.uint32
ALU = mybir.AluOpType
ACT = mybir.ActivationFunctionType
AX = mybir.AxisListType

P = 128
D = 1024
KB = D // P
SEQ, N_META, B_S = 256, 16, 8
L = SEQ + N_META
T = L + B_S
TAIL = T - 2 * P
TAIL_P = L - 2 * P
TILES = ((0, P), (P, P), (2 * P, TAIL))
CONV_W = 4
PAD = CONV_W - 1
N_HEADS, HEAD, N_KV = 16, 64, 2
GROUP = N_HEADS // N_KV
WINDOW = 128
OFF_Q, OFF_K = D, 2 * D
OFF_GR = OFF_K + 2 * N_KV * HEAD
OFF_GA = OFF_GR + D
E_N, TOP_K = 32, 4
LIMIT, ALPHA = 7.0, 1.702
EPS = 1e-6
LRU_C = 8.0
SLOPES = [2.0 ** (-8.0 * (h + 1) / N_HEADS) for h in range(N_HEADS)]

CAP = 64
PAIRS = E_N // 2
ROUNDS = -(-T // CAP)
NB = 512
RING = 16
EXTRA = 2
SLOT = 2048
UP_SLOTS = 2 * KB
PAIR_SLOTS = UP_SLOTS + KB
HALF = RING // 2
COLS = 256
W_IN_ORDER = ([OFF_K] + [COLS * i for i in range(4)] + [OFF_GR + COLS * i for i in range(4)]
              + [OFF_Q + COLS * i for i in range(4)] + [OFF_GA + COLS * i for i in range(4)])
N_WIN, N_WOUT = len(W_IN_ORDER), D * 2 // P // 2
TRUNK = N_WIN + N_WOUT
BLK_XR, BLK_GR, BLK_Q, BLK_GA = 2, 2 + KB, 2 + 2 * KB, 2 + 3 * KB

C_ID, C_IOTA = 0, P
C_KEEP = P + CAP * ROUNDS
C_DQ = C_KEEP
C_D2 = C_DQ + 3 * P
KEYS2 = L - P
C_DD = C_D2 + KEYS2
C_TRI = C_DD + P
C_SEL = C_TRI + P
C_SL2 = C_SEL + E_N
C_SLD = C_SL2 + N_KV
C_OH2 = C_SLD + 1
C_OHD = C_OH2 + N_KV * N_HEADS
C_END = C_OHD + N_HEADS
MASKED = -1e30


def shape_constants():
    c = np.zeros((P, C_END), np.float32)
    row = np.arange(P)[:, None]
    c[:, C_ID:C_ID + P] = np.eye(P)
    c[:, C_IOTA:C_KEEP] = np.arange(CAP * ROUNDS)

    def distances(dist):
        return np.where((dist >= 0) & (dist < WINDOW), -dist, MASKED)

    c[:, C_DQ:C_DQ + P] = distances(row - np.arange(P))
    c[:, C_DQ + P:C_D2] = distances(P + row - np.arange(2 * P))
    c[:, C_D2:C_DD] = distances(P + row % TAIL_P - np.arange(KEYS2))
    c[:, C_DD:C_TRI] = -(WINDOW - 1 - np.arange(P))
    c[:, C_TRI:C_SEL] = row < np.arange(P)
    c[:, C_SEL:C_SL2] = row % E_N == np.arange(E_N)
    for kv in range(N_KV):
        head = GROUP * kv + 2 * (row[:, 0] % 64 // 16) + row[:, 0] // 64
        c[:, C_SL2 + kv] = np.array(SLOPES)[head]
        c[:, C_OH2 + N_HEADS * kv:C_OH2 + N_HEADS * (kv + 1)] = head[:, None] == np.arange(N_HEADS)
    head = row[:, 0] % N_HEADS
    c[:, C_SLD] = np.array(SLOPES)[head]
    c[:, C_OHD:C_END] = head[:, None] == np.arange(N_HEADS)
    return c


def expert_load(i):
    return (i % 2, i // 2) if i < UP_SLOTS else ((i - UP_SLOTS) % 2, (i - UP_SLOTS) // 2)


def ring_place(n, start=False):
    m = n if start and n < RING else n - EXTRA
    slot = m % RING + HALF if m % RING < HALF else (m % RING + N_WIN) % HALF
    before = 0 if slot >= HALF else len(range(slot, TRUNK, HALF))
    return slot, m // RING, before


SEMS = """
x_loaded0 x_loaded1 x_loaded2 consts_loaded tables_loaded rows_loaded state_loaded wgate_loaded bias_loaded
extra_full0 extra_full1 fnorm_loaded router_loaded cache_loaded newkv_loaded zeroed consts_set squares tile_out
wr_scaled first_gather first_ready root rstd_ready xhat_ready vec_tr vec_ready h_tr h_evac_a h_evac_v proj_done
proj_evac xr_ready kv_tr kvtok_ready kd_tr kd_ready state_tr state_ready conv_step conv_ready sp_in sp_exp
sp_step gate_done gate_evac convout_tr convout_ready kc_tr kc_ready decay_ready tanh_ready ix_ready var_ready
mult_ready drive_ready rnn_gated bias_step score_done biased rowmax negmax sink_exp exp_done denom rden p_scaled
pt_done pt_evac_a pt_evac_v pv_done pv_evac qtok_tr qtok_ready qd_tr qd_ready dsc_done dsc_ready dst_done
q2_ready q2_done d_p_tr d_p_ready q2_p_tr q2_p_ready d_pv_done d_pv_ready q2_pv_done q2_pv_ready sinkcol_step
x_biased x_negmax x_sink_exp x_exp x_scaled ga_sig attn_gated wout_used hout_tr hout_ready tail_moved x2_ready
h2_ready h2_tr h2_evac logits_done negtop top_exp selb_ready rank_done flag_ready cast_ready gather_oh weight_oh
gather_done xt_ready up_done glu_ready lin_ready sig_ready gated_ready y_ready ytr_done yt_ready gwt_tr
gwt_ready down_done yd_ready combine_done added tail_copied tail_added ring_used window_stored convout_stored
hout_stored y_final stored router_step lru_step x_step
""".split()


def program(nc, c_in, x_prompt, x_sample, cache_k, cache_v, state_conv, state_h, meta_tokens, norm_mix, w_in, conv_w,
            conv_b, w_rg, b_rg, w_ig, b_ig, lru_lambda, attn_sinks, w_out, norm_ffn, w_router, b_router, w_up, b_up,
            w_down, b_down, norm_final,
            y_prompt, y_sample, new_k_p, new_v_p, new_conv_p, new_h_p, new_k_s, new_v_s, new_conv_s, new_h_s):
    ctx = ExitStack()
    with ctx:
        def sb(name, shape, dt=F32):
            return ctx.enter_context(nc.sbuf_tensor(name, shape, dt))

        s = namedtuple("Semaphores", SEMS)(*[ctx.enter_context(nc.semaphore(n)) for n in SEMS])
        ring_full = [ctx.enter_context(nc.semaphore(f"ring_full{i}")) for i in range(RING)]
        bank = [ctx.enter_context(nc.psum_tensor(f"bank{i}", [P, NB], F32)) for i in range(8)]

        ring = sb("ring", [P, RING, SLOT])
        x_tok = sb("x_tok", [P, 3, D])
        h_tok = sb("h_tok", [P, 3, D])
        keep = sb("keep", [P, C_KEEP])
        ident, iota = keep[:, C_ID:C_ID + P], keep[:, C_IOTA:C_KEEP]
        norm_b = sb("norm_b", [P, D])
        bias_parts = sb("bias_parts", [3 * E_N, 3 * D], BF16)
        pick = sb("pick", [3 * E_N, E_N, CAP], BF16)
        tri = sb("tri", [P, P], BF16)
        ones = sb("ones", [P, P], BF16)
        wr = sb("wr", [P, KB, E_N])
        br = sb("br", [P, E_N])
        vec = sb("vec", [P, 80])
        NRM, CW, CB, BR, BI, LAM, NFF = 0, 8, 40, 48, 56, 64, 72
        decay = sb("decay", [P, 2 * KB])
        h0 = sb("h0", [P, KB, B_S])
        sinks = sb("sinks", [P, N_HEADS])
        stat = sb("stat", [P, 16])
        eps = sb("eps", [P, 1])
        rank_m = sb("rank_m", [P, 3, E_N])
        wts = sb("wts", [P, 3, E_N])
        flag = sb("flag", [1, 1], I32)
        snk = sb("snk", [P, 4])

        area = sb("area", [P, (nc.sbuf_usable_end - nc.sbuf_base) // 4 // 8 * 8 - 8])
        used = [0]

        def at(base, shape, dt=F32, parts=P):
            size = int(np.prod(shape)) * (2 if dt == BF16 else 4) // 4
            v = area[0:parts, base:base + size]
            used[0] = max(used[0], base + size)
            if dt != F32:
                v = v.bitcast(dt)
            if len(shape) == 2:
                v = v.rearrange("p (a b) -> p a b", a=shape[0])
            elif len(shape) == 3:
                v = v.rearrange("p (a b c) -> p a b c", a=shape[0], b=shape[1])
            return v, base + size

        m_t, o = at(0, [2 * KB, T])
        kc, o = at(o, [B_S, P])
        vc, o = at(o, [B_S, P])
        kd, o = at(o, [N_KV, T])
        kt4, o = at(o, [3, 4 * HEAD])
        vt, o = at(o, [3, N_KV * HEAD])
        probs, o = at(o, [4, 3 * P])
        pt, o = at(o, [2, 3 * P])
        masks, o = at(o, [1, C_END - C_KEEP])
        q2z, o = at(o, [N_KV, P])
        qdz, o = at(o, [N_KV, GROUP * B_S])
        s_t, o = at(o, [1, P])
        p_d, o = at(o, [1, P])
        p_2, o = at(o, [N_KV, KEYS2])
        pt_d, o = at(o, [1, P])
        pt_2, o = at(o, [2 * N_KV, P])
        lru_tmp, o = at(o, [1, T])
        sm, o = at(o, [1, 64])
        masks, s_t, p_d, pt_d, lru_tmp, sm = (v[:, 0, :] for v in (masks, s_t, p_d, pt_d, lru_tmp, sm))
        st_in, o = at(0, [1, D])
        vec_in, o = at(o, [1, P])
        bias_in, o = at(o, [1, 3 * D])
        st_in, vec_in, bias_in = st_in[0:32, 0, :], vec_in[0:80, 0, :], bias_in[0:3 * E_N, 0, :]
        conv_out = probs[0:PAD + B_S, :, :].rearrange("p a b -> p (a b)")[:, 0:D]
        h2_t = m_t[:, 0:KB, :]
        o = 2 * KB * T
        lg, o = at(o, [3, E_N])
        top, o = at(o, [3, 8])
        topi, o = at(o, [3, 8], U32)
        topf, o = at(o, [3, TOP_K])
        ntop, o = at(o, [1, 4])
        tw, o = at(o, [3, TOP_K])
        tsum, o = at(o, [1, 4])
        eq, o = at(o, [3 * TOP_K, E_N])
        eqw, o = at(o, [3 * TOP_K, E_N])
        sel, o = at(o, [3, E_N])
        selb, o = at(o, [3, E_N], BF16)
        cnt, o = at(o, [1, 4])
        tail3, o = at(o, [3, D // 4])
        assert o <= 2 * KB * T + 2048
        ntop, tsum = ntop[:, 0, :], tsum[:, 0, :]
        o = 2 * KB * T + 2048
        g_oh, o = at(o, [3, P])
        gw0, o = at(o, [3, P])
        gw1, o = at(o, [3, P])
        xe, o = at(o, [KB, P])
        gw_t, o = at(o, [1, T])
        glu, o = at(o, [2, COLS])
        lin, o = at(o, [2, COLS])
        sig, o = at(o, [2, COLS])
        extra0, o = at(o, [1, SLOT])
        extra1, _ = at(2 * KB * T, [1, SLOT])
        extra = (extra0[:, 0, :], extra1[:, 0, :])
        o = 0
        y_e, o = at(o, [1, D])
        y_t, o = at(o, [KB, P])
        yd, o = at(o, [1, D])
        y_e, yd, gw_t = y_e[:, 0, :], yd[:, 0, :], gw_t[:, 0, :]
        tail_sb, o = at(o, [1, NB])
        tail_sb = tail_sb[:, 0, :]
        gw = (gw0, gw1)

        upper = ring[:, HALF:RING, :].rearrange("p a b -> p (a b)")
        o = 0

        def up(n, words=T):
            nonlocal o
            v = upper[:, o:o + n * words].rearrange("p (a b) -> p a b", a=n)
            o += n * words
            return v

        xr = up(KB, PAD + T)
        q_t = upper[:, 0:KB * T].rearrange("p (a b) -> p a b", a=KB)
        sdec = up(KB, PAD * B_S)
        g_r, g_a, xc, a_t, b_t, h_t = (up(KB) for _ in range(6))
        kv_t = g_a[:, 0:2, :]
        tanh_t = g_a
        wblk = h_tok[:, 0:2, :].rearrange("p a (j c) -> p a j c", j=KB)
        kc_t = h_tok[:, 2, :].rearrange("p (b c) -> p b c", b=B_S)
        q_tok = h_tok[0:B_S, 0, :].rearrange("p (g k d) -> p g k d", g=GROUP, k=N_KV)
        h_out = h_tok[0:1 + B_S, 1, :]

        win_v = w_in[0].rearrange("(k p) c -> p k c", p=P)
        wout_v = w_out[0].rearrange("(g j p) c -> g p j c", p=P, j=2)
        wup_v = w_up[0].rearrange("e (k p) c -> e k p c", p=P)
        wdn_v = w_down[0].rearrange("e (g j p) c -> e g p j c", p=P, j=2)

        def rows(t):
            return TILES[t][1]

        def msk(lo, n):
            return masks[:, lo - C_KEEP:lo - C_KEEP + n]

        def h2_bank(t, half):
            return bank[((5, 6), (0, 1), (7, 4))[t][half]][:, 0:4 * rows(t)]

        lg_bank = (bank[5], bank[6], bank[7])
        BY_END = (2, 0, 1)
        QUART = D // 4

        LAST_ORDER = (0, 2, 4, 1, 3)

        def combined_bank(unit, last):
            return bank[(0, 1, 2, 3, 6)[unit] if last else 6 + unit % 2]

        block = ctx.enter_context(nc.Block())

        @block.sync
        def _(eng):
            eng.dma_start(x_tok[0:N_META, 0, :], meta_tokens).then_inc(s.x_loaded0, 16)
            eng.dma_start(x_tok[N_META:P, 0, :], x_prompt[0, 0:P - N_META, :]).then_inc(s.x_loaded0, 16)
            eng.dma_start(x_tok[:, 1, :], x_prompt[0, P - N_META:2 * P - N_META, :]).then_inc(s.x_loaded1, 16)
            eng.dma_start(x_tok[0:TAIL_P, 2, :], x_prompt[0, 2 * P - N_META:SEQ, :]).then_inc(s.x_loaded2, 16)
            eng.dma_start(x_tok[TAIL_P:TAIL, 2, :], x_sample.rearrange("b o d -> (b o) d")).then_inc(s.x_loaded2, 16)
            for i, (v, n) in enumerate(((norm_mix, 1), (conv_w, 4), (conv_b, 1), (b_rg, 1), (b_ig, 1), (lru_lambda, 1),
                                        (norm_ffn, 1))):
                first = (NRM, CW, CB, BR, BI, LAM, NFF)[i]
                flat = v.rearrange("o (j c) -> (o j) c", c=P) if n == 1 else v.rearrange("o w (j c) -> (o w j) c", c=P)
                eng.dma_start(vec_in[first:first + KB * n, :], flat).then_inc(s.rows_loaded, 16)
            for n in range(TRUNK):
                if n == HALF:
                    eng.dma_start(masks[:, :], c_in[:, C_KEEP:C_END]).then_inc(s.tables_loaded, 16)
                    eng.dma_start(st_in[0:PAD * B_S, :], state_conv.rearrange("o b r d -> (o b r) d")).then_inc(s.state_loaded, 16)
                    eng.dma_start(st_in[PAD * B_S:32, :], state_h[0]).then_inc(s.state_loaded, 16)
                    for part in range(3):
                        eng.dma_start(bias_in[E_N * part:E_N * (part + 1), 0:2 * D], b_up[0]).then_inc(s.bias_loaded, 16)
                        eng.dma_start(bias_in[E_N * part:E_N * (part + 1), 2 * D:], b_down[0]).then_inc(s.bias_loaded, 16)
                    for cache, src in ((kc, cache_k), (vc, cache_v)):
                        eng.dma_start(cache[0:WINDOW - 1, :, :], src[0, :, 1:WINDOW].rearrange("b r k d -> r b (k d)"))\
                           .then_inc(s.cache_loaded, 16)
                    eng.dma_start(sinks[:, :], attn_sinks.to_broadcast([P, N_HEADS])).then_inc(s.tables_loaded, 16)
                    eng.dma_start(norm_b[:, :], norm_ffn.to_broadcast([P, D])).then_inc(s.router_loaded, 16)
                    eng.dma_start(wr[:, :, :], w_router[0].rearrange("(k p) e -> p k e", p=P)).then_inc(s.router_loaded, 16)
                    eng.dma_start(br[:, :], b_router.to_broadcast([P, E_N])).then_inc(s.router_loaded, 16)
                    eng.wait_ge(s.zeroed, 5)
                    for g, w in ((0, w_rg), (1, w_ig)):
                        for half in range(2):
                            eng.dma_start(wblk[64 * half:64 * half + 64, g, :, 64 * half:64 * half + 64],
                                          w[0].rearrange("(j h) c d -> h c j d", h=2)[half]).then_inc(s.wgate_loaded, 16)
                if n >= HALF:
                    eng.wait_ge(s.proj_done, 2 * (n - HALF) + 2)
                if n < N_WIN:
                    dst = ring[:, n % HALF, :].rearrange("p (k c) -> p k c", k=KB)
                    src = win_v[:, :, W_IN_ORDER[n]:W_IN_ORDER[n] + COLS]
                else:
                    dst = ring[:, n % HALF, :].rearrange("p (j c) -> p j c", j=2)
                    src = wout_v[n - N_WIN]
                eng.dma_start(dst, src).then_inc(ring_full[n % HALF], 16)
                if n == 10:
                    eng.wait_ge(s.kvtok_ready, 6)
                    for cache, tok, new in ((kc, kt4, new_k_p), (vc, vt, new_v_p)):
                        w = tok.rearrange("p t (k r) -> p t k r", k=N_KV)
                        first = L - WINDOW - P
                        out = new[0, 0]
                        for kv in range(N_KV):
                            eng.dma_start(out[0:P - first, kv, :], w[first:P, 1, kv, 0:HEAD]).then_inc(s.stored, 16)
                            eng.dma_start(out[P - first:WINDOW, kv, :], w[0:TAIL_P, 2, kv, 0:HEAD]).then_inc(s.stored, 16)
                            eng.dma_start(cache[WINDOW - 1:WINDOW, :, HEAD * kv:HEAD * (kv + 1)],
                                          w[TAIL_P:TAIL, 2, kv, 0:HEAD]).then_inc(s.newkv_loaded, 16)

            def expert_dma(expert, i, dst, full):
                part = expert_load(i)[1]
                if i < UP_SLOTS:
                    eng.dma_start(dst, wup_v[expert, part]).then_inc(full, 16)
                else:
                    eng.dma_start(dst.rearrange("p (j c) -> p j c", j=2), wdn_v[expert, part]).then_inc(full, 16)

            eng.wait_ge(s.attn_gated, KB)
            eng.wait_ge(s.rnn_gated, 1)
            eng.wait_ge(s.hout_tr, 2)
            for n in range(2 * PAIR_SLOTS):
                slot = ring_place(n, True)[0]
                dst, full = ring[:, slot, :], ring_full[slot]
                if HALF <= n < RING:
                    last = [m for m in range(TRUNK) if m % HALF == slot][-1]
                    eng.wait_ge(s.wout_used, last - N_WIN + 1)
                elif RING <= n < RING + EXTRA:
                    dst, full = extra[n - RING], (s.extra_full0, s.extra_full1)[n - RING]
                    if n == RING:
                        eng.wait_ge(s.h2_ready, 3)
                        eng.dma_start(norm_b[:, :], norm_final.rearrange("(o d) -> o d", o=1).to_broadcast([P, D]))\
                           .then_inc(s.fnorm_loaded, 16)
                    else:
                        eng.wait_ge(s.weight_oh, 1)
                elif n >= RING + EXTRA:
                    m = n - EXTRA - RING
                    eng.wait_ge(s.ring_used, (m if m < RING else m + EXTRA) + 1)
                expert_dma(2 * (n // PAIR_SLOTS) + expert_load(n % PAIR_SLOTS)[0], n % PAIR_SLOTS, dst, full)
            with eng.Fori(1, PAIRS // 2) as it:
                for n in range(2 * PAIR_SLOTS):
                    slot = ring_place(n)[0]
                    eng.wait_ge(s.ring_used, 2 * PAIR_SLOTS * it + (n - RING + 1))
                    expert_dma(4 * it + 2 * (n // PAIR_SLOTS) + expert_load(n % PAIR_SLOTS)[0], n % PAIR_SLOTS,
                               ring[:, slot, :], ring_full[slot])

            eng.wait_ge(s.flag_ready, 1)
            more = eng.value_load(flag[0:1, 0:1], min_val=0, max_val=1)
            with eng.If(more > 0):
                with eng.Fori(1, ROUNDS) as rnd:
                    with eng.Fori(0, PAIRS // 2) as it:
                        for n in range(2 * PAIR_SLOTS):
                            slot = ring_place(n)[0]
                            eng.wait_ge(s.ring_used, PAIR_SLOTS * PAIRS * rnd + 2 * PAIR_SLOTS * it + (n - RING + 1))
                            expert_dma(4 * it + 2 * (n // PAIR_SLOTS) + expert_load(n % PAIR_SLOTS)[0],
                                       n % PAIR_SLOTS, ring[:, slot, :], ring_full[slot])
            for step, t in enumerate(BY_END):
                eng.wait_ge(s.y_final, step + 1)
                if t == 0:
                    eng.dma_start(y_prompt[0, 0:P - N_META, :], h_tok[N_META:P, 0, :]).then_inc(s.stored, 16)
                elif t == 1:
                    for half, cols in enumerate((slice(0, NB), slice(NB, D))):
                        eng.wait_ge(s.y_final, step + half + 1)
                        eng.dma_start(y_prompt[0, P - N_META:2 * P - N_META, cols], h_tok[:, 1, cols]).then_inc(s.stored, 16)
                else:
                    eng.dma_start(y_prompt[0, 2 * P - N_META:SEQ, :], h_tok[0:TAIL_P, 2, :]).then_inc(s.stored, 16)
                    eng.dma_start(y_sample.rearrange("b o d -> (b o) d"), h_tok[TAIL_P:TAIL, 2, :]).then_inc(s.stored, 16)
            eng.wait_ge(s.stored, 16 * (8 + 1 + 5))
            eng.wait_ge(s.window_stored, 32)
            eng.wait_ge(s.convout_stored, 32)
            eng.wait_ge(s.hout_stored, 32)

        @block.gpsimd
        def _(eng):
            eng.memset(ones[:, :], 1.0).then_inc(s.zeroed, 1)
            eng.memset(xr[:, :, 0:PAD], 0.0).then_inc(s.zeroed, 1)
            eng.memset(q2z[:, :, :], 0.0).then_inc(s.zeroed, 1)
            eng.memset(qdz[:, :, :], 0.0).then_inc(s.zeroed, 1)
            eng.wait_ge(s.h_tr, KB)
            eng.memset(h_tok[:, 0:2, :], 0.0).then_inc(s.zeroed, 1)
            eng.wait_ge(s.bias_loaded, 16 * 6)
            eng.tensor_copy(bias_parts[:, :], bias_in[:, :]).then_inc(s.bias_step, 1)
            for part in range(1, 3):
                r = slice(0, E_N * (3 - part))
                eng.wait_ge(s.bias_step, 2 * part - 1)
                eng.tensor_tensor(bias_in[r, :], bias_in[r, :], bias_parts[r, :], ALU.subtract).then_inc(s.bias_step, 1)
                eng.wait_ge(s.bias_step, 2 * part)
                eng.tensor_copy(bias_parts[r, :], bias_in[r, :]).then_inc(s.bias_step, 1)
            eng.wait_ge(s.bias_step, 5)
            for j in range(KB):
                eng.wait_ge(s.gate_evac, 2 * j + 2)
                eng.wait_ge(s.ix_ready, j)
                eng.tensor_tensor(b_t[:, j, :], b_t[:, j, :], xc[:, j, :], ALU.mult).then_inc(s.ix_ready, 1)
            eng.wait_ge(s.ix_ready, KB)
            eng.wait_ge(s.lru_step, 2 * KB + 3)
            eng.tensor_tensor(m_t[:, 0:KB, :], g_r[:, :, :], xc[:, :, :], ALU.mult).then_inc(s.rnn_gated, 1)

        @block.scalar
        def _(eng):
            act = eng.activation
            eng.wait_ge(s.consts_set, 2)
            act(stat[:, 12:13], eps[:, :], ACT.Sqrt)
            eng.dma_start(keep[:, :], c_in[:, 0:C_KEEP]).then_inc(s.consts_loaded, 16)
            for t in range(3):
                eng.wait_ge((s.x_loaded0, s.x_loaded1, s.x_loaded2)[t], 32 if t != 1 else 16)
                act(h_tok[0:rows(t), t, :], x_tok[0:rows(t), t, :], ACT.Square, accum_out=stat[0:rows(t), t:t + 1])\
                    .then_inc(s.squares, 1)
                eng.wait_ge(s.squares, t + 1)
                act(stat[0:rows(t), 6 + t:7 + t], stat[0:rows(t), t:t + 1], ACT.Sqrt, bias=eps[0:rows(t), :],
                    scale=1.0 / D).then_inc(s.root, 1)
            eng.wait_ge(s.vec_ready, 1)
            for j in range(0, KB, 2):
                eng.wait_ge(s.h_tr, j + 1)
                act(h_t[:, j, :], bank[j][:, 0:T], ACT.Copy, scale=vec[:, NRM + j:NRM + j + 1]).then_inc(s.h_evac_a, 1)
            eng.wait_ge(s.sp_in, 1)
            act(sm[:, 8:16], sm[:, 0:8], ACT.Exp).then_inc(s.sp_exp, 1)

            def evac(n, dst, **kw):
                eng.wait_ge(s.proj_done, n + 1)
                return act(dst, bank[n % 2][:, 0:T], kw.pop("func", ACT.Copy), **kw)

            evac(0, kv_t[:, 0, :]).then_inc(s.proj_evac, 1)
            evac(1, kv_t[:, 1, :]).then_inc(s.proj_evac, 1)
            eng.wait_ge(s.zeroed, 2)
            for j in range(KB):
                evac(BLK_XR + j, xr[:, j, PAD:PAD + T]).then_inc(s.xr_ready, 1)
                act(xc[:, j, :], bank[j % 2][:, 0:T], ACT.Identity, bias=vec[:, CB + j:CB + j + 1],
                    scale=vec[:, CW + 8 * PAD + j:CW + 8 * PAD + j + 1]).then_inc(s.proj_evac, 1)
                if j == 2:
                    for kv in range(N_KV):
                        eng.wait_ge(s.kd_tr, kv + 1)
                        act(kd[:, kv, :], bank[6 + kv][:, 0:T], ACT.Copy).then_inc(s.kd_ready, 1)
            for j in range(KB):
                evac(BLK_GR + j, g_r[:, j, :], func=ACT.Sigmoid).then_inc(s.proj_evac, 1)
                for g, (dst, b) in enumerate(((a_t, BR), (b_t, BI))):
                    eng.wait_ge(s.gate_done, 2 * j + g + 1)
                    act(dst[:, j, :], bank[4 + g][:, 0:T], ACT.Sigmoid, bias=vec[:, b + j:b + j + 1])\
                        .then_inc(s.gate_evac, 1)
                if j == 5 or j == 6:
                    half = j - 5
                    eng.wait_ge(s.kc_tr, half + 1)
                    act(kc_t[:, 4 * half:4 * half + 4, :].rearrange("p b c -> p (b c)"), bank[6 + half][:, :], ACT.Copy)\
                        .then_inc(s.kc_ready, 1)
            eng.wait_ge(s.convout_ready, 2)
            eng.dma_start(new_conv_p[0, 0], conv_out[0:PAD, :]).then_inc(s.convout_stored, 16)
            eng.dma_start(new_conv_s[0, :, PAD - 1, :], conv_out[PAD:PAD + B_S, :]).then_inc(s.convout_stored, 16)
            eng.dma_start(new_conv_s[0, :, 0:PAD - 1, :], state_conv[0, :, 1:PAD, :]).then_inc(s.stored, 16)
            eng.wait_ge(s.cache_loaded, 32)
            eng.wait_ge(s.newkv_loaded, 64)
            for cache, new in ((kc, new_k_s), (vc, new_v_s)):
                eng.dma_start(new[0].rearrange("b r k d -> r b (k d)"), cache[:, :, :]).then_inc(s.window_stored, 16)
            eng.wait_ge(s.gate_evac, 2 * KB)

            def attention_exp(j):
                for p in range(2):
                    col = 16 * (j % 2) + 8 * p
                    h = 2 * j + p
                    eng.wait_ge(s.negmax, h + 1)
                    act(sm[:, col + 4:col + 6], sm[:, col + 2:col + 4], ACT.Exp, bias=sinks[:, h:h + 1])\
                        .then_inc(s.sink_exp, 1)
                    buf = probs[:, 2 * (j % 2) + p, :]
                    for i, (lo, hi) in enumerate(((0, P), (P, 3 * P))):
                        act(buf[:, lo:hi], buf[:, lo:hi], ACT.Exp, bias=sm[:, col + 2 + i:col + 3 + i],
                            accum_out=sm[:, col + i:col + i + 1]).then_inc(s.exp_done, 1)

            def extra_exp(n, buf, width):
                col = 32 + 6 * n
                eng.wait_ge(s.x_negmax, n + 1)
                act(sm[:, col + 2:col + 3], sm[:, col + 1:col + 2], ACT.Exp, bias=snk[:, n:n + 1])\
                    .then_inc(s.x_sink_exp, 1)
                act(buf[:, 0:width], buf[:, 0:width], ACT.Exp, bias=sm[:, col + 1:col + 2],
                    accum_out=sm[:, col:col + 1]).then_inc(s.x_exp, 1)

            for st in range(2 * KB):
                j = st % KB
                if st < 2:
                    for i in range(4 * st, 4 * st + 4):
                        act(tanh_t[:, i, :], a_t[:, i, :], ACT.Tanh, scale=decay[:, i:i + 1]).then_inc(s.tanh_ready, 1)
                        eng.wait_ge(s.tanh_ready, i + 1)
                        act(a_t[:, i, :], a_t[:, i, :], ACT.Exp, scale=decay[:, KB + i:KB + i + 1]).then_inc(s.decay_ready, 1)
                if st < KB:
                    if st == 0:
                        eng.wait_ge(s.conv_ready, KB)
                        eng.wait_ge(s.convout_tr, 2)
                    evac(BLK_Q + j, q_t[:, j, :], scale=HEAD ** -0.5).then_inc(s.proj_evac, 1)
                else:
                    if st == KB:
                        eng.wait_ge(s.drive_ready, 1)
                    evac(BLK_GA + j, g_a[:, j, :]).then_inc(s.proj_evac, 1)
                if st == 2:
                    eng.wait_ge(s.var_ready, KB)
                    act(tanh_t[:, :, :], tanh_t[:, :, :], ACT.Sqrt).then_inc(s.mult_ready, 1)
                if st % 2 == 1:
                    if st >= 3:
                        eng.wait_ge(s.pt_done, 2 * (st // 2 - 1) + 1)
                        if st >= 5:
                            eng.wait_ge(s.pv_done, st // 2 - 1)
                        act(pt[:, 0, :], bank[6][:, 0:3 * P], ACT.Copy).then_inc(s.pt_evac_a, 1)
                    if st == 7:
                        for half in range(2):
                            eng.wait_ge(s.qtok_tr, half + 1)
                            act(q_tok[:, :, half, :], bank[4 + half][0:B_S, :].rearrange("p (g d) -> p g d", g=GROUP),
                                ACT.Copy).then_inc(s.qtok_ready, 1)
                    attention_exp(st // 2)
                if st >= 4 and st % 2 == 0:
                    jj = (st - 4) // 2
                    eng.wait_ge(s.pv_done, jj + 1)
                    act(m_t[:, KB + jj, 0:2 * P], bank[5][:, 0:2 * P], ACT.Copy).then_inc(s.pv_evac, 1)
                if st == 9:
                    extra_exp(0, p_2[:, 0, :], KEYS2)
                    extra_exp(1, p_2[:, 1, :], KEYS2)
                if st == 10:
                    extra_exp(2, p_d, P)
                if st == 13:
                    eng.wait_ge(s.q2_p_tr, 1)
                    act(pt_2[:, 0:2, :].rearrange("p a b -> p (a b)"), bank[5][:, 0:2 * P], ACT.Copy)\
                        .then_inc(s.q2_p_ready, 1)
                    act(pt_2[0:16, 2:4, :].rearrange("p a b -> p (a b)"), bank[5][0:16, 2 * P:4 * P], ACT.Copy)\
                        .then_inc(s.q2_p_ready, 1)
                    eng.wait_ge(s.d_p_tr, 1)
                    act(pt_d[:, :], bank[4][:, 0:P], ACT.Copy).then_inc(s.d_p_ready, 1)
                if st == 14:
                    eng.wait_ge(s.d_pv_done, 1)
                    act(m_t[:, KB:2 * KB, L:T], bank[4][:, 0:KB * B_S].rearrange("p (j b) -> p j b", j=KB), ACT.Copy)\
                        .then_inc(s.d_pv_ready, 1)
                if st == 15:
                    eng.wait_ge(s.q2_pv_done, 1)
                    act(m_t[:, KB:2 * KB, 2 * P:L], bank[4][:, 0:KB * 16].rearrange("p (j q) -> p j q", j=KB), ACT.Copy)\
                        .then_inc(s.q2_pv_ready, 1)
            eng.wait_ge(s.pv_done, KB - 1)
            act(m_t[:, 2 * KB - 2, 0:2 * P], bank[5][:, 0:2 * P], ACT.Copy).then_inc(s.pv_evac, 1)
            eng.wait_ge(s.pt_done, 2 * (KB - 1) + 1)
            act(pt[:, 0, :], bank[6][:, 0:3 * P], ACT.Copy).then_inc(s.pt_evac_a, 1)
            eng.wait_ge(s.pv_done, KB)
            act(m_t[:, 2 * KB - 1, 0:2 * P], bank[5][:, 0:2 * P], ACT.Copy).then_inc(s.pv_evac, 1)
            eng.wait_ge(s.proj_evac, 2 + 4 * KB)
            for half in range(2):
                r = slice(4 * half, 4 * half + 4)
                act(g_a[:, r, :], g_a[:, r, :], ACT.Sigmoid).then_inc(s.ga_sig, 1)
            for half in range(2):
                eng.wait_ge(s.hout_tr, half + 1)
                act(h_out[:, NB * half:NB * (half + 1)], bank[6 + half][0:1 + B_S, :], ACT.Copy).then_inc(s.hout_ready, 1)
            act(stat[:, 13:14], eps[:, :], ACT.Sqrt)
            eng.wait_ge(s.hout_ready, 2)
            eng.dma_start(new_h_p[0], h_out[0:1, :]).then_inc(s.hout_stored, 16)
            eng.dma_start(new_h_s[0], h_out[1:1 + B_S, :]).then_inc(s.hout_stored, 16)
            def h2_copies(t, step):
                n = rows(t)
                for half in range(2):
                    eng.wait_ge(s.h2_tr, 2 * step + half + 1)
                    act(h2_t[:, 4 * half:4 * half + 4, P * t:P * t + n],
                        h2_bank(t, half).rearrange("p (j c) -> p j c", j=4), ACT.Copy).then_inc(s.h2_evac, 1)

            eng.wait_ge(s.window_stored, 32)
            for step, t in enumerate(BY_END):
                n = rows(t)
                if t == 2:
                    eng.wait_ge(s.tile_out, 1)
                    for c in range(1, 4):
                        act(tail3[0:n, c - 1, :], bank[4][32 * c:32 * c + n, 0:QUART], ACT.Copy).then_inc(s.tail_moved, 1)
                elif t == 1:
                    eng.wait_ge(s.hout_stored, 32)
                    h2_copies(2, 0)
                    h2_copies(0, 1)
                eng.wait_ge(s.x2_ready, 2 * step + 2)
                act(h_tok[0:n, t, :], x_tok[0:n, t, :], ACT.Square, accum_out=stat[0:n, t:t + 1]).then_inc(s.squares, 1)
                eng.wait_ge(s.squares, 3 + step + 1)
                act(stat[0:n, 6 + t:7 + t], stat[0:n, t:t + 1], ACT.Sqrt, bias=eps[0:n, :], scale=1.0 / D)\
                    .then_inc(s.root, 1)
            h2_copies(1, 2)
            for step, t in enumerate(BY_END):
                n = rows(t)
                eng.wait_ge(s.negtop, step + 1)
                act(tw[0:n, t, :], top[0:n, t, 0:TOP_K], ACT.Exp, bias=ntop[0:n, t:t + 1],
                    accum_out=tsum[0:n, t:t + 1]).then_inc(s.top_exp, 1)

            def yd_copy(q):
                eng.wait_ge(s.combine_done, 5 * q)
                for c in range(2):
                    if c == 0:
                        eng.wait_ge(s.down_done, q + 1)
                    else:
                        eng.wait_ge(s.ring_used, PAIR_SLOTS * q + PAIR_SLOTS)
                    act(yd[:, NB * c:NB * (c + 1)], bank[4 + c][:, :], ACT.Copy).then_inc(s.yd_ready, 1)

            def sigmoid(q, n):
                eng.wait_ge(s.glu_ready, 4 * q + (n + 1))
                if n < 2:
                    eng.wait_ge(s.y_ready, 4 * q)
                else:
                    eng.wait_ge(s.y_ready, 4 * q + (n - 1))
                act(sig[:, n % 2, :], glu[:, n % 2, :], ACT.Sigmoid, scale=ALPHA).then_inc(s.sig_ready, 1)

            def xe_copy(q, half):
                eng.wait_ge(s.gather_done, 2 * q + (half + 1))
                act(xe[:, 4 * half:4 * half + 4, :].rearrange("p a b -> p (a b)"), bank[6 + half][:, :], ACT.Copy)\
                    .then_inc(s.xt_ready, 1)

            def gwt_copy(q):
                eng.wait_ge(s.gwt_tr, q + 1)
                eng.wait_ge(s.combine_done, 5 * q)
                act(gw_t[:, :], bank[4][:, 0:T], ACT.Copy).then_inc(s.gwt_ready, 1)

            def yt_copy(q):
                for half in range(2):
                    eng.wait_ge(s.ytr_done, 2 * q + (half + 1))
                    act(y_t[:, 4 * half:4 * half + 4, :].rearrange("p a b -> p (a b)"), bank[6 + half][:, :], ACT.Copy)\
                        .then_inc(s.yt_ready, 1)

            def pair(q, gather_next):
                sigmoid(q, 0)
                sigmoid(q, 1)
                if gather_next:
                    xe_copy(q + 1, 0)
                sigmoid(q, 2)
                sigmoid(q, 3)
                if gather_next:
                    xe_copy(q + 1, 1)
                gwt_copy(q)
                yt_copy(q)
                yd_copy(q)

            eng.wait_ge(s.first_gather, 1)
            act(xe[:, 0:2, :].rearrange("p a b -> p (a b)"), bank[6][:, 0:2 * P], ACT.Copy).then_inc(s.first_ready, 1)
            eng.wait_ge(s.gather_done, 1)
            act(xe[:, 2:4, :].rearrange("p a b -> p (a b)"), bank[6][:, 2 * P:4 * P], ACT.Copy).then_inc(s.xt_ready, 1)
            xe_copy(0, 1)
            pair(0, True)
            pair(1, True)
            with eng.Fori(1, PAIRS // 2 - 1) as it:
                pair(2 * it, True)
                pair(2 * it + 1, True)
            pair(PAIRS - 2, True)
            pair(PAIRS - 1, False)
            more = eng.value_load(flag[0:1, 0:1], min_val=0, max_val=1)
            with eng.If(more > 0):
                with eng.Fori(PAIRS // 2, PAIRS // 2 * ROUNDS) as it:
                    for u in range(2):
                        xe_copy(2 * it + u, 0)
                        xe_copy(2 * it + u, 1)
                        pair(2 * it + u, False)
                eng.wait_ge(s.added, 5 * PAIRS * ROUNDS)
                eng.wait_ge(s.tail_added, PAIRS * ROUNDS)
            act(stat[:, 14:15], eps[:, :], ACT.Sqrt)
            for step, t in enumerate(BY_END):
                if step == 0:
                    eng.wait_ge(s.tail_added, PAIRS)
                else:
                    eng.wait_ge(s.added, 5 * (PAIRS - 1) + step + 3)
                act(ring[0:rows(t), t, 0:D], x_tok[0:rows(t), t, :], ACT.Square, accum_out=stat[0:rows(t), t:t + 1])\
                    .then_inc(s.squares, 1)
                eng.wait_ge(s.squares, 6 + step + 1)
                act(stat[0:rows(t), 6 + t:7 + t], stat[0:rows(t), t:t + 1], ACT.Sqrt, bias=eps[0:rows(t), :],
                    scale=1.0 / D).then_inc(s.root, 1)

        @block.tensor
        def _(eng):
            mm = eng.matmul

            def keep_warm(n, b):
                for _ in range(n):
                    mm(b[:, :], ones[:, :], ones[:, 0:1].to_broadcast([P, NB]), start=True, stop=True)

            eng.wait_ge(s.zeroed, 1)
            keep_warm(22, bank[7])
            eng.wait_ge(s.consts_loaded, 16)
            for j in range(KB):
                if j == 4:
                    eng.wait_ge(s.rows_loaded, 16 * 7)
                    eng.transpose(bank[7][:, 0:80], vec_in[:, :], ident[0:80, 0:80]).then_inc(s.vec_tr, 1)
                if j == 7:
                    eng.wait_ge(s.vec_ready, 1)
                for t, (lo, n) in enumerate(TILES):
                    if j == 0:
                        eng.wait_ge(s.xhat_ready, t + 1)
                    tr = eng.transpose(bank[j][:, lo:lo + n], h_tok[0:n, t, P * j:P * (j + 1)], ident[0:n, 0:n])
                tr.then_inc(s.h_tr, 1)

            def scores(j):
                eng.wait_ge(s.proj_evac, BLK_Q + j + 1)
                eng.wait_ge(s.kd_ready, 2)
                eng.wait_ge(s.biased, 2 * j)
                kv = j // 4
                for lo, n in ((0, P), (P, 2 * P)):
                    for p in range(2):
                        h = slice(64 * p, 64 * p + 64)
                        m = mm(bank[2 + p][:, lo:lo + n], q_t[h, j, lo:lo + P], kd[h, kv, 0:n], start=True, stop=True)
                m.then_inc(s.score_done, 1)

            def p_transposes(j):
                eng.wait_ge(s.pt_evac_a, j)
                eng.wait_ge(s.pt_evac_v, j)
                for p in range(2):
                    eng.wait_ge(s.p_scaled, 2 * (2 * j + p) + 2)
                    for c in range(3):
                        tr = eng.transpose(bank[6 + p][:, P * c:P * (c + 1)], probs[:, 2 * (j % 2) + p, P * c:P * (c + 1)],
                                           ident)
                    tr.then_inc(s.pt_done, 1)

            def pv(j):
                eng.wait_ge(s.pt_evac_a, j + 1)
                eng.wait_ge(s.pt_evac_v, j + 1)
                eng.wait_ge(s.pv_evac, j)
                v = slice(64 * (j // 4), 64 * (j // 4) + 64)
                for p in range(2):
                    mm(bank[5][64 * p:64 * p + 64, 0:2 * P], vt[:, 0, v], pt[:, p, 0:2 * P], start=True, stop=False)
                for p in range(2):
                    m = mm(bank[5][64 * p:64 * p + 64, P:2 * P], vt[:, 1, v], pt[:, p, 2 * P:3 * P], start=False, stop=True)
                m.then_inc(s.pv_done, 1)

            def after_kv():
                eng.wait_ge(s.proj_evac, 2)
                for i in range(2):
                    for t, (lo, n) in enumerate(TILES):
                        tr = eng.transpose(bank[6 + i][0:n, P * t:P * (t + 1)], kv_t[:, i, lo:lo + n], ident)
                    tr.then_inc(s.kv_tr, 1)

            def keys_major():
                eng.wait_ge(s.kvtok_ready, 6)
                for kv in range(N_KV):
                    for t, (lo, n) in enumerate(TILES):
                        tr = eng.transpose(bank[6 + kv][:, lo:lo + n], kt4[0:n, t, P * kv:P * (kv + 1)], ident[0:n, 0:n])
                    tr.then_inc(s.kd_tr, 1)

            def states():
                eng.wait_ge(s.kd_ready, 2)
                eng.wait_ge(s.state_loaded, 32)
                for j in range(KB):
                    tr = eng.transpose(bank[6][:, 32 * j:32 * (j + 1)], st_in[:, P * j:P * (j + 1)], ident[0:32, 0:32])
                tr.then_inc(s.state_tr, 1)

            def gates(j):
                eng.wait_ge(s.conv_ready, j + 1)
                eng.wait_ge(s.wgate_loaded, 64)
                for g in range(2):
                    if j:
                        eng.wait_ge(s.gate_evac, 2 * j - 1 + g)
                    mm(bank[4 + g][:, 0:T], wblk[:, g, j, :], xc[:, j, :], start=True, stop=True).then_inc(s.gate_done, 1)

            def conv_rows(half):
                eng.wait_ge(s.state_ready, 2)
                eng.wait_ge(s.xr_ready, KB)
                for i in range(4):
                    tr = eng.transpose(bank[6 + half][0:PAD + B_S, P * i:P * (i + 1)], xr[:, 4 * half + i, L:PAD + T], ident)
                tr.then_inc(s.convout_tr, 1)

            def window_keys(half):
                eng.wait_ge(s.convout_ready, half + 1)
                eng.wait_ge(s.cache_loaded, 32)
                eng.wait_ge(s.newkv_loaded, 64)
                for i in range(4):
                    tr = eng.transpose(bank[6 + half][:, P * i:P * (i + 1)], kc[:, 4 * half + i, :], ident)
                tr.then_inc(s.kc_tr, 1)

            def sample_queries():
                eng.wait_ge(s.proj_evac, BLK_Q + KB)
                eng.wait_ge(s.pv_evac, 2)
                for half in range(2):
                    for i in range(4):
                        tr = eng.transpose(bank[4 + half][0:B_S, P * i:P * (i + 1)], q_t[:, 4 * half + i, L:T], ident)
                    tr.then_inc(s.qtok_tr, 1)

            def sample_heads():
                eng.wait_ge(s.qtok_ready, 2)
                for g in range(GROUP):
                    tr = eng.transpose(bank[4][:, B_S * g:B_S * (g + 1)], q_tok[:, g, :, :].rearrange("b k d -> b (k d)"),
                                       ident[0:B_S, 0:B_S])
                tr.then_inc(s.qd_tr, 1)

            def sample_scores():
                eng.wait_ge(s.qd_ready, 2)
                eng.wait_ge(s.kc_ready, 2)
                qd = qdz.rearrange("p k (g b) -> p k g b", g=GROUP)
                for b in range(B_S):
                    m = mm(bank[4][:, N_HEADS * b:N_HEADS * (b + 1)], kc_t[:, b, :], qd[:, :, :, b], start=True, stop=True)
                m.then_inc(s.dsc_done, 1)

            def last_scores():
                eng.wait_ge(s.q2_ready, 4)
                eng.wait_ge(s.pv_evac, 3)
                for kv in range(N_KV):
                    m = mm(bank[5][:, KEYS2 * kv:KEYS2 * (kv + 1)], q2z[:, kv, :], kd[:, kv, P:L], start=True, stop=True)
                m.then_inc(s.q2_done, 1)

            def sample_rows():
                eng.wait_ge(s.dsc_ready, 1)
                eng.transpose(bank[4][:, 0:P], s_t, ident).then_inc(s.dst_done, 1)

            def sample_p():
                eng.wait_ge(s.x_scaled, 3)
                eng.transpose(bank[4][:, 0:P], p_d, ident).then_inc(s.d_p_tr, 1)

            def last_p():
                eng.wait_ge(s.pv_evac, 5)
                for kv in range(N_KV):
                    eng.transpose(bank[5][:, P * kv:P * (kv + 1)], p_2[:, kv, 0:P], ident)
                for kv in range(N_KV):
                    tr = eng.transpose(bank[5][0:TAIL_P, P * (2 + kv):P * (3 + kv)], p_2[:, kv, P:KEYS2], ident)
                tr.then_inc(s.q2_p_tr, 1)

            def sample_pv():
                eng.wait_ge(s.d_p_ready, 1)
                out = bank[4][:, 0:KB * B_S].rearrange("p (j b) -> p j b", j=KB)
                pr = pt_d.rearrange("p (b k i r) -> p b k i r", b=B_S, k=N_KV, r=2)
                for b in range(B_S):
                    for kv in range(N_KV):
                        for p in range(2):
                            m = mm(out[64 * p:64 * p + 64, 4 * kv:4 * kv + 4, b], vc[:, b, HEAD * kv:HEAD * (kv + 1)],
                                   pr[:, b, kv, :, p], start=True, stop=True)
                m.then_inc(s.d_pv_done, 1)

            def last_pv():
                eng.wait_ge(s.q2_p_ready, 2)
                eng.wait_ge(s.d_pv_ready, 1)
                for kv in range(N_KV):
                    v = slice(HEAD * kv, HEAD * (kv + 1))
                    for p in range(2):
                        o, r = slice(64 * p, 64 * p + 64), slice(64 * p, 64 * p + 64)
                        mm(bank[4][o, 64 * kv:64 * kv + 64], vt[:, 1, v], pt_2[:, kv, r], start=True, stop=False)
                        m = mm(bank[4][o, 64 * kv:64 * kv + 64], vt[0:TAIL_P, 2, v], pt_2[0:TAIL_P, 2 + kv, r],
                               start=False, stop=True)
                m.then_inc(s.q2_pv_done, 1)

            for n in range(2 * N_WIN):
                if n % 2 == 0:
                    g = n // 2
                    eng.wait_ge(ring_full[g % HALF], 16 * (g // HALF + 1))
                    w = ring[:, g % HALF, :].rearrange("p (k c) -> p k c", k=KB)
                if n >= 2:
                    eng.wait_ge(s.proj_evac, n - 1)
                for k in range(KB):
                    if n == 0:
                        eng.wait_ge(s.h_evac_v if k % 2 else s.h_evac_a, k // 2 + 1)
                    m = mm(bank[n % 2][:, 0:T], w[:, k, P * (n % 2):P * (n % 2) + P], h_t[:, k, :],
                           start=(k == 0), stop=(k == KB - 1))
                m.then_inc(s.proj_done, 1)
                {1: after_kv, 3: keys_major, 5: states}.get(n, lambda: None)()
                if BLK_GR <= n < BLK_Q:
                    j = n - BLK_GR
                    gates(j)
                    if j in (3, 4):
                        conv_rows(j - 3)
                    if j in (5, 6):
                        window_keys(j - 5)
                st = n - BLK_Q
                if st < 0:
                    continue
                if st == 3:
                    eng.wait_ge(s.kc_ready, 2)
                if st % 2 == 1:
                    scores(st // 2)
                    if st >= 3:
                        p_transposes(st // 2 - 1)
                elif st >= 4:
                    if st == 8:
                        eng.wait_ge(s.qtok_ready, 2)
                    if st == 10:
                        eng.wait_ge(s.x_biased, 2)
                    if st == 14:
                        eng.wait_ge(s.q2_p_ready, 2)
                    pv((st - 4) // 2)
                if st == 7:
                    sample_queries()
                elif st == 8:
                    sample_heads()
                elif st == 9:
                    sample_scores()
                    last_scores()
                elif st == 10:
                    sample_rows()
                elif st == 13:
                    last_p()
                    sample_p()
                elif st == 14:
                    sample_pv()
                elif st == 15:
                    last_pv()

            eng.wait_ge(s.proj_evac, 2 * N_WIN)
            eng.wait_ge(s.rnn_gated, 1)
            def out_product(g, t):
                lo, rn = TILES[t]
                w = ring[:, (N_WIN + g) % HALF, :].rearrange("p (j c) -> p j c", j=2)
                for j in range(2):
                    k = 2 * g + j
                    for c in range(4 if t == 2 else 2):
                        out = bank[4][32 * c:32 * c + rn, 0:QUART] if t == 2 else bank[2 * t + c][:, :]
                        n = QUART if t == 2 else NB
                        m = mm(out, m_t[:, k, lo:lo + rn], w[:, j, n * c:n * (c + 1)], start=(k == 0),
                               stop=(k == 2 * KB - 1), tile_position=(0, 32 * c) if t == 2 else None)
                return m

            def h2_transposes(t, step):
                n = rows(t)
                eng.wait_ge(s.x2_ready, 2 * step + 2)
                for half in range(2):
                    for i in range(4):
                        j = 4 * half + i
                        tr = eng.transpose(h2_bank(t, half)[:, n * i:n * (i + 1)], x_tok[0:n, t, P * j:P * (j + 1)],
                                           ident[0:n, 0:n])
                    tr.then_inc(s.h2_tr, 1)

            def logits(t, step):
                lo, n = TILES[t]
                eng.wait_ge(s.h2_evac, 2 * step + 2)
                for k in range(KB):
                    m = mm(lg_bank[t][0:n, 0:E_N], h2_t[:, k, lo:lo + n], wr[:, k, :],
                           start=(k == 0), stop=(k == KB - 1))
                m.then_inc(s.logits_done, 1)

            for g in range(N_WOUT // 2):
                n = N_WIN + g
                eng.wait_ge(ring_full[n % HALF], 16 * (n // HALF + 1))
                for t in (0, 2, 1):
                    if g == 0 and t == 2:
                        eng.wait_ge(s.q2_pv_ready, 1)
                    if g == 0 and t == 1:
                        eng.wait_ge(s.biased, N_HEADS)
                    m = out_product(g, t)
                m.then_inc(s.wout_used, 1)
                if g == 0:
                    pv(KB - 2)
                    p_transposes(KB - 1)
                if g == 1:
                    pv(KB - 1)
                if g == 2:
                    eng.wait_ge(s.pt_evac_a, KB)
                    eng.wait_ge(s.pt_evac_v, KB)
                    for half in range(2):
                        for i in range(4):
                            tr = eng.transpose(bank[6 + half][0:1 + B_S, P * i:P * (i + 1)],
                                               xc[:, 4 * half + i, L - 1:T], ident)
                        tr.then_inc(s.hout_tr, 1)
            for step, t in enumerate(BY_END):
                for g in range(N_WOUT // 2, N_WOUT):
                    if step == 0:
                        n = N_WIN + g
                        eng.wait_ge(ring_full[n % HALF], 16 * (n // HALF + 1))
                        eng.wait_ge(s.attn_gated, 2 * (g - 4) + 2)
                    if step == 2 and g == N_WOUT - 1:
                        eng.wait_ge(s.pv_evac, KB)
                        eng.wait_ge(s.hout_ready, 2)
                        h2_transposes(2, 0)
                        h2_transposes(0, 1)
                    m = out_product(g, t)
                    if step == 2:
                        m.then_inc(s.wout_used, 1)
                if step < 2:
                    m.then_inc(s.tile_out, 1)
            eng.wait_ge(s.wr_scaled, 1)
            logits(2, 0)
            logits(0, 1)
            h2_transposes(1, 2)
            logits(1, 2)
            keep_warm(7, bank[2])
            eng.wait_ge(s.selb_ready, 1)
            eng.wait_ge(s.cast_ready, 2)
            eng.wait_ge(s.zeroed, 1)
            for t in range(3):
                for t2 in range(t + 1):
                    mm(bank[3][:, E_N * t:E_N * (t + 1)], tri[:, :] if t2 == t else ones[:, :], selb[:, t2, :],
                       start=(t2 == 0), stop=(t2 == t))
            for t in range(3):
                m = mm(bank[3][0:1, 3 * E_N:4 * E_N], ones[:, 0:1], selb[:, t, :], start=(t == 0), stop=(t == 2))
            m.then_inc(s.rank_done, 1)
            keep_warm(7, bank[2])

            def gather(q, combined, blocks):
                eng.wait_ge(s.gather_oh, q + 1)
                if combined is not None:
                    eng.wait_ge(s.added, 5 * combined)
                for j in blocks:
                    for t, (lo, n) in enumerate(TILES):
                        m = mm(bank[6 + j // 4][:, P * (j % 4):P * (j % 4 + 1)], h_tok[0:n, t, P * j:P * (j + 1)],
                               g_oh[0:n, t, :], start=(t == 0), stop=(t == 2))
                return m

            def gather_all(q, combined):
                for half in range(2):
                    gather(q, combined, range(4 * half, 4 * half + 4)).then_inc(s.gather_done, 1)

            def combine(q, unit, last=False):
                if unit == 0:
                    eng.wait_ge(s.gwt_ready, q + 1)
                    eng.wait_ge(s.yd_ready, 2 * q + (1 if last else 2))
                elif unit == 4 and last:
                    eng.wait_ge(s.yd_ready, 2 * q + 2)
                elif unit >= 2 and not last:
                    eng.wait_ge(s.added, 5 * q + (unit - 1))
                b = combined_bank(unit, last)
                if unit < 4:
                    lo, c = P * (unit // 2), unit % 2
                    m = mm(b[:, :], gw_t[:, lo:lo + P], yd[:, NB * c:NB * (c + 1)], start=True, stop=True)
                else:
                    for c in range(2):
                        m = mm(b[64 * c:64 * c + TAIL, :], gw_t[:, 2 * P:T], yd[:, NB * c:NB * (c + 1)],
                               start=True, stop=True)
                m.then_inc(s.combine_done, 1)

            def full(u, i, it):
                n = PAIR_SLOTS * u + i
                start = isinstance(it, int) and it == 0
                if start and RING <= n < RING + EXTRA:
                    eng.wait_ge((s.extra_full0, s.extra_full1)[n - RING], 16)
                    return extra[n - RING]
                slot, turn, before = ring_place(n, start)
                eng.wait_ge(ring_full[slot], 48 * it + 16 * (turn + before + 1))
                return ring[:, slot, :]

            def pair(q, u, it, pq, pipelined, first=False, last=False):
                chosen = pick[:, bass.ds(2 * pq, 2), :].rearrange("p e c -> p (e c)")
                if first:
                    gather(q, None, (0, 1)).then_inc(s.first_gather, 1)
                    eng.wait_ge(s.flag_ready, 1)
                else:
                    eng.wait_ge(s.y_ready, 4 * q)
                    eng.wait_ge(s.xt_ready, 2 * q + 2)
                for n in range(4):
                    mm(bank[n][:, :], chosen, bias_parts[:, NB * n:NB * (n + 1)], start=True, stop=False,
                       skip_group_check=True)
                for k in range(KB):
                    if first and k == 0:
                        eng.wait_ge(s.first_ready, 1)
                    elif first and k == 1:
                        gather(q, None, (2, 3)).then_inc(s.gather_done, 1)
                    elif first and k == 2:
                        eng.wait_ge(s.xt_ready, 1)
                    elif first and k == 3:
                        gather(q, None, range(4, KB)).then_inc(s.gather_done, 1)
                    elif first and k == KB // 2:
                        eng.wait_ge(s.xt_ready, 2)
                    w = [full(u, 2 * k + e, it) for e in range(2)]
                    for n in range(4):
                        for e in range(2):
                            m = mm(bank[n][64 * e:64 * e + 64, :], xe[:, k, 64 * e:64 * e + 64],
                                   w[e][:, NB * n:NB * (n + 1)], start=False, stop=(k == KB - 1), skip_group_check=True)
                            if n == 3:
                                m.then_inc(s.ring_used, 1)
                            elif k == KB - 1 and e == 1:
                                m.then_inc(s.up_done, 1)
                    if pipelined and not first and 1 <= k <= 5:
                        combine(q - 1, k - 1)
                if pipelined and not last:
                    gather_all(q + 1, None if first else q)
                eng.wait_ge(s.weight_oh, q + 1)
                eng.wait_ge(s.yd_ready, 2 * q)
                for t, (lo, n) in enumerate(TILES):
                    tr = eng.transpose(bank[4][:, lo:lo + n], gw[u][0:n, t, :], ident[0:n, 0:n])
                tr.then_inc(s.gwt_tr, 1)
                if pipelined and not last:
                    eng.wait_ge(s.xt_ready, 2 * q + 4)
                elif pipelined:
                    eng.wait_ge(s.added, 5 * q)
                for half in range(2):
                    eng.wait_ge(s.y_ready, 4 * q + (2 * half + 2))
                    for i in range(4):
                        tr = eng.transpose(bank[6 + half][:, P * i:P * (i + 1)],
                                           y_e[:, P * (4 * half + i):P * (4 * half + i + 1)], ident)
                    tr.then_inc(s.ytr_done, 1)
                eng.wait_ge(s.gwt_ready, q + 1)
                for c in range(2):
                    mm(bank[4 + c][:, :], chosen, bias_parts[:, NB * (4 + c):NB * (5 + c)], start=True, stop=False,
                       skip_group_check=True)
                for fp in range(KB // 2):
                    if fp % 2 == 0:
                        eng.wait_ge(s.yt_ready, 2 * q + (fp // 2 + 1))
                    if last and fp >= 2:
                        keep_warm(6, bank[2])
                    w = [full(u, UP_SLOTS + 2 * fp + e, it) for e in range(2)]
                    for c in range(2):
                        for j in range(2):
                            for e in range(2):
                                f = 2 * fp + j
                                m = mm(bank[4 + c][64 * e:64 * e + 64, :], y_t[:, f, 64 * e:64 * e + 64],
                                       w[e][:, D * j + NB * c:D * j + NB * (c + 1)], start=False, stop=(f == KB - 1),
                                       skip_group_check=True)
                                if j == 1 and c == 1:
                                    m.then_inc(s.ring_used, 1)
                                elif f == KB - 1 and e == 1:
                                    m.then_inc(s.down_done, 1)

            pair(0, 0, 0, 0, True, first=True)
            pair(1, 1, 0, 1, True)
            with eng.Fori(1, PAIRS // 2 - 1) as it:
                for u in range(2):
                    pair(2 * it + u, u, it, 2 * it + u, True)
            pair(PAIRS - 2, 0, PAIRS // 2 - 1, PAIRS - 2, True)
            pair(PAIRS - 1, 1, PAIRS // 2 - 1, PAIRS - 1, True, last=True)
            for unit in LAST_ORDER:
                combine(PAIRS - 1, unit, True)
            eng.wait_ge(s.flag_ready, 1)
            more = eng.value_load(flag[0:1, 0:1], min_val=0, max_val=1)
            with eng.If(more > 0):
                with eng.Fori(1, ROUNDS) as rnd:
                    with eng.Fori(0, PAIRS // 2) as i2:
                        for u in range(2):
                            it = PAIRS // 2 * rnd + i2
                            q = 2 * it + u
                            gather_all(q, q)
                            pair(q, u, it, 2 * i2 + u, False)
                            for unit in range(5):
                                combine(q, unit)

        @block.vector
        def _(eng):
            eng.memset(stat[:, :], 1.0).then_inc(s.consts_set, 1)
            eng.memset(eps[:, :], EPS).then_inc(s.consts_set, 1)
            for t in range(3):
                n = rows(t)
                eng.wait_ge(s.root, t + 1)
                eng.reciprocal(stat[0:n, 9 + t:10 + t], stat[0:n, 6 + t:7 + t]).then_inc(s.rstd_ready, 1)
                eng.wait_ge(s.rstd_ready, t + 1)
                eng.tensor_scalar(h_tok[0:n, t, :], x_tok[0:n, t, :], stat[0:n, 9 + t:10 + t], None, ALU.mult)\
                   .then_inc(s.xhat_ready, 1)
            eng.wait_ge(s.vec_tr, 1)
            eng.tensor_copy(vec[:, :], bank[7][:, 0:80]).then_inc(s.vec_ready, 1)
            eng.wait_ge(s.vec_ready, 1)
            for j in range(1, KB, 2):
                eng.wait_ge(s.h_tr, j + 1)
                eng.tensor_scalar(h_t[:, j, :], bank[j][:, 0:T], vec[:, NRM + j:NRM + j + 1], None, ALU.mult)\
                   .then_inc(s.h_evac_v, 1)
            def stepper(sem):
                done = 0

                def step(ins):
                    nonlocal done
                    ins.then_inc(sem, 1)
                    done += 1
                    eng.wait_ge(sem, done)
                return step

            lam = vec[:, LAM:LAM + KB]
            v = [sm[:, 16 + 8 * i:24 + 8 * i] for i in range(5)]
            step = stepper(s.sp_step)
            step(eng.tensor_scalar(v[0], lam, -1.0, None, ALU.mult))
            step(eng.tensor_tensor(v[1], v[0], lam, ALU.min))
            eng.tensor_copy(sm[:, 0:8], v[1]).then_inc(s.sp_in, 1)
            eng.wait_ge(s.sp_exp, 1)
            e = sm[:, 8:16]
            step(eng.tensor_scalar(v[1], e, 2.0, None, ALU.add))
            step(eng.reciprocal(v[1], v[1]))
            step(eng.tensor_tensor(v[1], v[1], e, ALU.mult))
            step(eng.tensor_tensor(v[2], v[1], v[1], ALU.mult))
            step(eng.tensor_scalar(v[3], v[2], 1.0 / 17, None, ALU.mult))
            for k in range(7, 0, -1):
                step(eng.scalar_tensor_tensor(out=v[3], in0=v[3], scalar=1.0 / (2 * k + 1), in1=v[2],
                                              op0=ALU.add, op1=ALU.mult))
            step(eng.scalar_tensor_tensor(out=v[3], in0=v[3], scalar=1.0, in1=v[1], op0=ALU.add, op1=ALU.mult))
            step(eng.tensor_scalar(v[0], v[0], 0.0, LRU_C, ALU.max, ALU.mult))
            step(eng.scalar_tensor_tensor(out=decay[:, 0:KB], in0=v[3], scalar=2 * LRU_C, in1=v[0],
                                          op0=ALU.mult, op1=ALU.add))
            step(eng.tensor_scalar(decay[:, KB:2 * KB], decay[:, 0:KB], -1.0, None, ALU.mult))
            for i in range(2):
                eng.wait_ge(s.kv_tr, i + 1)
                src = bank[6 + i][:, 0:3 * P].rearrange("p (t k d) -> p t k d", t=3, k=N_KV)
                for dup in range(2 - i):
                    dst = (kt4.rearrange("p t (k r d) -> p t k r d", k=N_KV, r=2)[:, :, :, dup, :] if i == 0
                           else vt.rearrange("p t (k d) -> p t k d", k=N_KV))
                    eng.tensor_copy(dst[:, 0:2], src[:, 0:2]).then_inc(s.kvtok_ready, 1)
                    eng.tensor_copy(dst[0:TAIL, 2], src[0:TAIL, 2]).then_inc(s.kvtok_ready, 1)
            eng.wait_ge(s.state_tr, 1)
            st = bank[6][:, 0:32 * KB].rearrange("p (j r) -> p j r", j=KB)
            eng.tensor_copy(sdec[:, :, :], st[:, :, 0:PAD * B_S]).then_inc(s.state_ready, 1)
            eng.tensor_copy(h0[:, :, :], st[:, :, PAD * B_S:32]).then_inc(s.state_ready, 1)
            eng.wait_ge(s.state_ready, 2)
            eng.wait_ge(s.tables_loaded, 32)
            eng.tensor_copy(tri[:, :], msk(C_TRI, P)).then_inc(s.cast_ready, 1)
            eng.tensor_copy(pick[:, :, :], masks[0:3 * E_N, C_SEL - C_KEEP:C_SEL - C_KEEP + E_N].unsqueeze(2)
                            .to_broadcast([3 * E_N, E_N, CAP])).then_inc(s.cast_ready, 1)
            for n, c in enumerate((C_OH2, C_OH2 + N_HEADS, C_OHD)):
                eng.tensor_tensor(msk(c, N_HEADS), msk(c, N_HEADS), sinks[:, :], ALU.mult).then_inc(s.sinkcol_step, 1)
                eng.wait_ge(s.sinkcol_step, 2 * n + 1)
                eng.tensor_reduce(snk[:, n:n + 1], msk(c, N_HEADS), AX.X, ALU.add).then_inc(s.sinkcol_step, 1)
            n = 0
            for j in range(KB):
                eng.wait_ge(s.proj_evac, BLK_XR + j + 1)
                old = sdec[:, j, :].rearrange("p (b r) -> p b r", r=PAD)
                for i in range(PAD):
                    w = vec[:, CW + KB * i + j:CW + KB * i + j + 1]
                    if i:
                        eng.wait_ge(s.conv_step, n)
                    eng.scalar_tensor_tensor(out=xc[:, j, 0:L], in0=xr[:, j, i:i + L], scalar=w, in1=xc[:, j, 0:L],
                                             op0=ALU.mult, op1=ALU.add).then_inc(s.conv_step, 1)
                    ins = eng.scalar_tensor_tensor(out=xc[:, j, L:T], in0=old[:, :, i], scalar=w, in1=xc[:, j, L:T],
                                                   op0=ALU.mult, op1=ALU.add)
                    if i < PAD - 1:
                        ins.then_inc(s.conv_step, 1)
                        n += 2
                    else:
                        ins.then_inc(s.conv_ready, 1)
                        n += 1
            for half in range(2):
                eng.wait_ge(s.convout_tr, half + 1)
                eng.tensor_copy(conv_out[:, NB * half:NB * (half + 1)], bank[6 + half][0:PAD + B_S, :])\
                   .then_inc(s.convout_ready, 1)

            def attention_bias(j):
                eng.wait_ge(s.score_done, j + 1)
                if j >= 2:
                    eng.wait_ge(s.pt_done, 2 * (j - 1))
                for p in range(2):
                    h = 2 * j + p
                    buf, col = probs[:, 2 * (j % 2) + p, :], 16 * (j % 2) + 8 * p
                    eng.scalar_tensor_tensor(out=buf, in0=msk(C_DQ, 3 * P), scalar=SLOPES[h], in1=bank[2 + p][:, 0:3 * P],
                                             op0=ALU.mult, op1=ALU.add).then_inc(s.biased, 1)
                if j >= 2:
                    pt_copy(j - 1)
                for p in range(2):
                    h = 2 * j + p
                    buf, col = probs[:, 2 * (j % 2) + p, :], 16 * (j % 2) + 8 * p
                    eng.wait_ge(s.biased, h + 1)
                    eng.tensor_reduce(sm[:, col + 2:col + 3], buf[:, 0:P], AX.X, ALU.max).then_inc(s.rowmax, 1)
                    eng.tensor_reduce(sm[:, col + 3:col + 4], buf[:, P:3 * P], AX.X, ALU.max).then_inc(s.rowmax, 1)
                for p in range(2):
                    h = 2 * j + p
                    col = 16 * (j % 2) + 8 * p
                    eng.wait_ge(s.rowmax, 2 * h + 2)
                    eng.tensor_scalar(sm[:, col + 2:col + 4], sm[:, col + 2:col + 4], sinks[:, h:h + 1], -1.0,
                                      ALU.max, ALU.mult).then_inc(s.negmax, 1)

            def attention_sum(j):
                for p in range(2):
                    h = 2 * j + p
                    col = 16 * (j % 2) + 8 * p
                    eng.wait_ge(s.exp_done, 2 * h + 2)
                    eng.wait_ge(s.sink_exp, h + 1)
                    eng.tensor_tensor(sm[:, col + 4:col + 6], sm[:, col + 4:col + 6], sm[:, col:col + 2], ALU.add)\
                       .then_inc(s.denom, 1)
                    eng.wait_ge(s.denom, h + 1)
                    eng.reciprocal(sm[:, col + 6:col + 8], sm[:, col + 4:col + 6]).then_inc(s.rden, 1)
                for p in range(2):
                    buf, col = probs[:, 2 * (j % 2) + p, :], 16 * (j % 2) + 8 * p
                    eng.wait_ge(s.rden, 2 * j + p + 1)
                    eng.tensor_scalar(buf[:, 0:P], buf[:, 0:P], sm[:, col + 6:col + 7], None, ALU.mult)\
                       .then_inc(s.p_scaled, 1)
                    eng.tensor_scalar(buf[:, P:3 * P], buf[:, P:3 * P], sm[:, col + 7:col + 8], None, ALU.mult)\
                       .then_inc(s.p_scaled, 1)

            def pt_copy(j):
                eng.wait_ge(s.pt_done, 2 * j + 2)
                eng.wait_ge(s.pv_done, j)
                eng.tensor_copy(pt[:, 1, :], bank[7][:, 0:3 * P]).then_inc(s.pt_evac_v, 1)

            def extra_bias(n, buf, width, dist, slope, scores):
                col = 32 + 6 * n
                eng.scalar_tensor_tensor(out=buf, in0=dist, scalar=slope, in1=scores, op0=ALU.mult, op1=ALU.add)\
                   .then_inc(s.x_biased, 1)
                eng.wait_ge(s.x_biased, n + 1)
                eng.tensor_reduce(sm[:, col + 1:col + 2], buf, AX.X, ALU.max).then_inc(s.x_step, 1)
                eng.wait_ge(s.x_step, (1, 2, 7)[n])
                eng.tensor_scalar(sm[:, col + 1:col + 2], sm[:, col + 1:col + 2], snk[:, n:n + 1], -1.0,
                                  ALU.max, ALU.mult).then_inc(s.x_negmax, 1)

            def extra_sum(n, buf):
                col = 32 + 6 * n
                eng.wait_ge(s.x_exp, n + 1)
                eng.wait_ge(s.x_sink_exp, n + 1)
                eng.tensor_tensor(sm[:, col + 2:col + 3], sm[:, col + 2:col + 3], sm[:, col:col + 1], ALU.add)\
                   .then_inc(s.x_step, 1)
                eng.wait_ge(s.x_step, (3, 5, 8)[n])
                eng.reciprocal(sm[:, col + 3:col + 4], sm[:, col + 2:col + 3]).then_inc(s.x_step, 1)
                eng.wait_ge(s.x_step, (4, 6, 9)[n])
                eng.tensor_scalar(buf, buf, sm[:, col + 3:col + 4], None, ALU.mult).then_inc(s.x_scaled, 1)

            for j in range(KB):
                eng.wait_ge(s.decay_ready, j + 1)
                if j:
                    eng.wait_ge(s.var_ready, j)
                eng.tensor_tensor(lru_tmp, a_t[:, j, :], a_t[:, j, :], ALU.mult).then_inc(s.lru_step, 1)
                eng.wait_ge(s.lru_step, j + 1)
                eng.scalar_tensor_tensor(out=tanh_t[:, j, :], in0=lru_tmp, scalar=1.0, in1=tanh_t[:, j, :],
                                         op0=ALU.add, op1=ALU.mult).then_inc(s.var_ready, 1)
            eng.wait_ge(s.convout_stored, 32)
            attention_bias(0)
            attention_sum(0)
            pt_copy(0)
            eng.wait_ge(s.mult_ready, 1)
            eng.wait_ge(s.ix_ready, KB)
            eng.memset(tanh_t[:, :, 0:1], 1.0).then_inc(s.lru_step, 1)
            eng.wait_ge(s.lru_step, KB + 1)
            eng.tensor_tensor(b_t[:, :, :], b_t[:, :, :], tanh_t[:, :, :], ALU.mult).then_inc(s.drive_ready, 1)
            eng.wait_ge(s.drive_ready, 1)
            attention_bias(1)
            attention_sum(1)
            for j in range(KB):
                eng.tensor_tensor_scan(xc[:, j, 0:L], a_t[:, j, 0:L], b_t[:, j, 0:L], 0.0, ALU.mult, ALU.add)\
                   .then_inc(s.lru_step, 1)
            eng.tensor_tensor(h0[:, :, :], h0[:, :, :], a_t[:, :, L:T], ALU.mult).then_inc(s.lru_step, 1)
            eng.wait_ge(s.lru_step, 2 * KB + 2)
            eng.tensor_tensor(xc[:, :, L:T], h0[:, :, :], b_t[:, :, L:T], ALU.add).then_inc(s.lru_step, 1)
            eng.wait_ge(s.lru_step, 2 * KB + 3)
            for j in range(2, KB):
                attention_bias(j)
                if j == 3:
                    eng.wait_ge(s.proj_evac, BLK_Q + KB)
                    eng.wait_ge(s.zeroed, 4)
                    for kv in range(N_KV):
                        for p in range(2):
                            eng.tensor_copy(q2z[64 * p:64 * p + 64, kv, 64 * p:64 * p + 64]
                                            .rearrange("p (i q) -> p i q", i=4),
                                            q_t[64 * p:64 * p + 64, 4 * kv:4 * kv + 4, 2 * P:L]).then_inc(s.q2_ready, 1)
                    attention_sum(j)
                    eng.wait_ge(s.qd_tr, 1)
                    for kv in range(N_KV):
                        h = slice(64 * kv, 64 * kv + 64)
                        eng.tensor_copy(qdz[h, kv, :], bank[4][h, 0:GROUP * B_S]).then_inc(s.qd_ready, 1)
                elif j == 4:
                    attention_sum(j)
                    eng.wait_ge(s.dsc_done, 1)
                    eng.tensor_copy(s_t, bank[4][:, 0:P]).then_inc(s.dsc_ready, 1)
                    eng.wait_ge(s.q2_done, 1)
                    for kv in range(N_KV):
                        extra_bias(kv, p_2[:, kv, :], KEYS2, msk(C_D2, KEYS2), msk(C_SL2 + kv, 1),
                                   bank[5][:, KEYS2 * kv:KEYS2 * (kv + 1)])
                    for kv in range(N_KV):
                        extra_sum(kv, p_2[:, kv, :])
                    eng.wait_ge(s.dst_done, 1)
                    extra_bias(2, p_d, P, msk(C_DD, P), msk(C_SLD, 1), bank[4][:, 0:P])
                elif j == 5:
                    attention_sum(j)
                    extra_sum(2, p_d)
                else:
                    attention_sum(j)
            pt_copy(KB - 1)
            eng.wait_ge(s.d_pv_ready, 1)
            eng.wait_ge(s.q2_pv_ready, 1)
            for j in range(KB):
                eng.wait_ge(s.pv_evac, j + 1)
                eng.wait_ge(s.ga_sig, j // 4 + 1)
                eng.tensor_tensor(m_t[:, KB + j, :], m_t[:, KB + j, :], g_a[:, j, :], ALU.mult).then_inc(s.attn_gated, 1)

            eng.wait_ge(s.window_stored, 32)
            router_step = stepper(s.router_step)
            router_step(eng.memset(topf[:, :, :], -1.0))
            router_step(eng.memset(tw[:, :, :], 0.0))

            def residual(t, step):
                n = rows(t)
                if step < 2:
                    eng.wait_ge(s.tile_out, step + 1)
                else:
                    eng.wait_ge(s.wout_used, N_WOUT)
                for c in range(2):
                    if t == 2:
                        cols = slice(0, QUART) if c == 0 else slice(QUART, D)
                        if c == 1:
                            eng.wait_ge(s.tail_moved, 3)
                        src = bank[4][0:n, 0:QUART] if c == 0 else tail3[0:n, :, :].rearrange("p a b -> p (a b)")
                    else:
                        cols = slice(NB * c, NB * (c + 1))
                        src = bank[2 * t + c][0:n, :]
                    x = x_tok[0:n, t, cols]
                    eng.tensor_tensor(x, x, src, ALU.add).then_inc(s.x2_ready, 1)

            def normalise(t, step):
                n = rows(t)
                eng.wait_ge(s.root, 3 + step + 1)
                eng.reciprocal(stat[0:n, 9 + t:10 + t], stat[0:n, 6 + t:7 + t]).then_inc(s.rstd_ready, 1)
                eng.wait_ge(s.rstd_ready, 3 + step + 1)
                eng.scalar_tensor_tensor(out=h_tok[0:n, t, :], in0=x_tok[0:n, t, :], scalar=stat[0:n, 9 + t:10 + t],
                                         in1=norm_b[0:n, :], op0=ALU.mult, op1=ALU.mult).then_inc(s.h2_ready, 1)

            eng.wait_ge(s.router_loaded, 48)
            eng.tensor_tensor(wr[:, :, :], wr[:, :, :], vec[:, NFF:NFF + KB].unsqueeze(2).to_broadcast([P, KB, E_N]),
                              ALU.mult).then_inc(s.wr_scaled, 1)
            for step, t in enumerate(BY_END):
                residual(t, step)
                normalise(t, step)
            for step, t in enumerate(BY_END):
                n = rows(t)
                eng.wait_ge(s.logits_done, step + 1)
                router_step(eng.scalar_tensor_tensor(out=lg[0:n, t, :], in0=lg_bank[t][0:n, 0:E_N],
                                                     scalar=stat[0:n, 9 + t:10 + t], in1=br[0:n, :],
                                                     op0=ALU.mult, op1=ALU.add))
                router_step(eng.max(top[0:n, t, :], lg[0:n, t, :]))
                eng.tensor_scalar(ntop[0:n, t:t + 1], top[0:n, t, 0:1], -1.0, None, ALU.mult).then_inc(s.negtop, 1)
                router_step(eng.max_index(topi[0:n, t, :], top[0:n, t, :], lg[0:n, t, :]))
                router_step(eng.tensor_copy(topf[0:n, t, :], topi[0:n, t, 0:TOP_K]))
            flat = [P, 3 * TOP_K, E_N]
            router_step(eng.tensor_tensor(eq[:, :, :], iota[:, 0:E_N].unsqueeze(1).to_broadcast(flat),
                                          topf.rearrange("p t k -> p (t k)").unsqueeze(2).to_broadcast(flat),
                                          ALU.is_equal))
            router_step(eng.tensor_reduce(sel[:, :, :], eq.rearrange("p (t k) e -> p t e k", t=3), AX.X, ALU.add))
            eng.tensor_copy(selb[:, :, :], sel[:, :, :]).then_inc(s.selb_ready, 1)
            eng.wait_ge(s.rank_done, 1)
            router_step(eng.scalar_tensor_tensor(out=rank_m[:, :, :], in0=bank[3][:, 0:3 * E_N]
                                                 .rearrange("p (t e) -> p t e", t=3), scalar=1.0, in1=sel[:, :, :],
                                                 op0=ALU.add, op1=ALU.mult))
            router_step(eng.tensor_scalar(rank_m[:, :, :], rank_m[:, :, :], -1.0, None, ALU.add))
            shape = [P, 3, 2, CAP]
            view = "p t (e c) -> p t e c"

            def gather_hots(q, pq, slots):
                rk = rank_m[:, :, bass.ds(2 * pq, 2)].unsqueeze(3).to_broadcast(shape)
                eng.wait_ge(s.gather_done, 2 * q)
                eng.wait_ge(s.weight_oh, q)
                eng.tensor_tensor(g_oh.rearrange(view, e=2), slots.unsqueeze(1).unsqueeze(1).to_broadcast(shape), rk,
                                  ALU.is_equal).then_inc(s.gather_oh, 1)

            def weight_hots(q, u, pq, reused):
                wt = wts[:, :, bass.ds(2 * pq, 2)].unsqueeze(3).to_broadcast(shape)
                eng.wait_ge(s.gather_oh, q + 1)
                if reused:
                    eng.wait_ge(s.gwt_tr, q - 1)
                eng.tensor_tensor(gw[u].rearrange(view, e=2), g_oh.rearrange(view, e=2), wt, ALU.mult)\
                   .then_inc(s.weight_oh, 1)

            def one_hots(q, u, pq, slots, reused):
                gather_hots(q, pq, slots)
                weight_hots(q, u, pq, reused)

            def add(q, last=False):
                eng.wait_ge(s.added, 5 * q)
                eng.wait_ge(s.tail_added, q)
                for step, unit in enumerate(LAST_ORDER if last else range(5)):
                    eng.wait_ge(s.combine_done, 5 * q + (step + 1))
                    b = combined_bank(unit, last)
                    if unit < 4:
                        x = x_tok[:, unit // 2, NB * (unit % 2):NB * (unit % 2 + 1)]
                        eng.tensor_tensor(x, x, b[:, :], ALU.add).then_inc(s.added, 1)
                    else:
                        eng.tensor_copy(tail_sb[0:TAIL, :], b[64:64 + TAIL, :]).then_inc(s.tail_copied, 1)
                        x = x_tok[0:TAIL, 2, 0:NB]
                        eng.tensor_tensor(x, x, b[0:TAIL, :], ALU.add).then_inc(s.added, 1)
                        eng.wait_ge(s.tail_copied, q + 1)
                        x = x_tok[0:TAIL, 2, NB:D]
                        eng.tensor_tensor(x, x, tail_sb[0:TAIL, :], ALU.add).then_inc(s.tail_added, 1)

            def gating(q):
                def clamp(n):
                    if n < 3:
                        eng.wait_ge(s.up_done, 3 * q + (n + 1))
                    else:
                        eng.wait_ge(s.ring_used, PAIR_SLOTS * q + UP_SLOTS)
                    eng.wait_ge(s.y_ready, 4 * q + (n - 1 if n > 1 else 0))
                    z = bank[n][:, :].rearrange("p (f two) -> p f two", two=2)
                    eng.tensor_scalar(glu[:, n % 2, :], z[:, :, 0], LIMIT, None, ALU.min).then_inc(s.glu_ready, 1)
                    eng.tensor_scalar(lin[:, n % 2, :], z[:, :, 1], LIMIT, -LIMIT, ALU.min, ALU.max)\
                       .then_inc(s.lin_ready, 1)
                    eng.wait_ge(s.lin_ready, 4 * q + (n + 1))
                    eng.scalar_tensor_tensor(out=lin[:, n % 2, :], in0=lin[:, n % 2, :], scalar=1.0, in1=glu[:, n % 2, :],
                                             op0=ALU.add, op1=ALU.mult).then_inc(s.gated_ready, 1)

                def finish(n):
                    eng.wait_ge(s.gated_ready, 4 * q + (n + 1))
                    eng.wait_ge(s.sig_ready, 4 * q + (n + 1))
                    if n == 0:
                        eng.wait_ge(s.ytr_done, 2 * q)
                    eng.tensor_tensor(y_e[:, COLS * n:COLS * (n + 1)], lin[:, n % 2, :], sig[:, n % 2, :], ALU.mult)\
                       .then_inc(s.y_ready, 1)

                clamp(0)
                for n in range(1, 4):
                    clamp(n)
                    finish(n - 1)
                finish(3)

            first = iota[:, 0:CAP]
            gather_hots(0, 0, first)
            router_step(eng.tensor_reduce(cnt[0:1, 0, 0:1], bank[3][0:1, 3 * E_N:4 * E_N], AX.X, ALU.max))
            eng.tensor_scalar(flag[:, :], cnt[0:1, 0, 0:1], float(CAP), None, ALU.is_gt).then_inc(s.flag_ready, 1)
            for step, t in enumerate(BY_END):
                n = rows(t)
                eng.wait_ge(s.top_exp, step + 1)
                router_step(eng.reciprocal(tsum[0:n, t:t + 1], tsum[0:n, t:t + 1]))
                router_step(eng.tensor_scalar(tw[0:n, t, :], tw[0:n, t, :], tsum[0:n, t:t + 1], None, ALU.mult))
            router_step(eng.tensor_tensor(eqw[:, :, :], eq[:, :, :],
                                          tw.rearrange("p t k -> p (t k)").unsqueeze(2).to_broadcast(flat), ALU.mult))
            router_step(eng.tensor_reduce(wts[:, :, :], eqw.rearrange("p (t k) e -> p t e k", t=3), AX.X, ALU.add))
            weight_hots(0, 0, 0, False)
            one_hots(1, 1, 1, first, False)
            gating(0)
            one_hots(2, 0, 2, first, True)
            add(0)
            gating(1)
            with eng.Fori(1, PAIRS // 2 - 1) as it:
                for u in range(2):
                    q = 2 * it + u
                    one_hots(q + 1, 1 - u, q + 1, first, True)
                    add(q - 1)
                    gating(q)
            one_hots(PAIRS - 1, 1, PAIRS - 1, first, True)
            add(PAIRS - 3)
            gating(PAIRS - 2)
            add(PAIRS - 2)
            gating(PAIRS - 1)
            add(PAIRS - 1, True)
            more = eng.value_load(flag[0:1, 0:1], min_val=0, max_val=1)
            with eng.If(more > 0):
                with eng.Fori(1, ROUNDS) as rnd:
                    with eng.Fori(0, PAIRS // 2) as i2:
                        for u in range(2):
                            q = PAIRS * rnd + 2 * i2 + u
                            one_hots(q, u, 2 * i2 + u, iota[:, bass.ds(CAP * rnd, CAP)], True)
                            gating(q)
                            add(q)
            eng.wait_ge(s.fnorm_loaded, 16)
            for step, t in enumerate(BY_END):
                n = rows(t)
                eng.wait_ge(s.root, 6 + step + 1)
                eng.reciprocal(stat[0:n, 9 + t:10 + t], stat[0:n, 6 + t:7 + t]).then_inc(s.rstd_ready, 1)
                eng.wait_ge(s.rstd_ready, 6 + step + 1)
                for cols in ((slice(0, NB), slice(NB, D)) if step == 2 else (slice(0, D),)):
                    eng.scalar_tensor_tensor(out=h_tok[0:n, t, cols], in0=x_tok[0:n, t, cols],
                                             scalar=stat[0:n, 9 + t:10 + t], in1=norm_b[0:n, cols],
                                             op0=ALU.mult, op1=ALU.mult).then_inc(s.y_final, 1)


INPUTS = ["x_prompt", "x_sample", "cache_k", "cache_v", "state_conv", "state_h", "meta_tokens", "norm_mix", "w_in",
          "conv_w", "conv_b", "w_rg", "b_rg", "w_ig", "b_ig", "lru_lambda", "attn_sinks", "w_out", "norm_ffn",
          "w_router", "b_router", "w_up", "b_up", "w_down", "b_down", "norm_final"]
OUTPUTS = [("y_prompt", (1, SEQ, D)), ("y_sample", (B_S, 1, D)),
           ("new_k_prompt", (1, 1, WINDOW, N_KV, HEAD)), ("new_v_prompt", (1, 1, WINDOW, N_KV, HEAD)),
           ("new_conv_prompt", (1, 1, PAD, D)), ("new_h_prompt", (1, 1, D)),
           ("new_k_sample", (1, B_S, WINDOW, N_KV, HEAD)), ("new_v_sample", (1, B_S, WINDOW, N_KV, HEAD)),
           ("new_conv_sample", (1, B_S, PAD, D)), ("new_h_sample", (1, B_S, D))]


def kernel(**inputs):
    import concourse.bacc as bacc
    from concourse.bass_utils import run_bass_kernel_spmd

    nc = bacc.Bacc("TRN2", target_bir_lowering=False, num_devices=1, dynamic_dma_scratch_size=64)
    arrays = {"in_constants": shape_constants()}
    for name in INPUTS:
        arrays["in_" + name] = np.ascontiguousarray(inputs[name])
    args = [nc.dram_tensor(n, a.shape, mybir.dt.from_np(a.dtype), kind="ExternalInput").ap() for n, a in arrays.items()]
    args += [nc.dram_tensor("out_" + n, shape, F32, kind="ExternalOutput").ap() for n, shape in OUTPUTS]
    program(nc, *args)
    result = run_bass_kernel_spmd(nc, [arrays], core_ids=[0]).results[0]
    return tuple(result["out_" + n] for n, _ in OUTPUTS)
```
